# Optimizing a Trainium2 kernel written in Bass

```python
import jax, jax.numpy as jnp
from jax import lax
import numpy as np

D_MODEL = 1024
BATCH = 1
SEQ = 1024
DEPTH = 2

N_MIXERS = 2
FOX_HEADS = 16
FOX_HEAD_DIM = D_MODEL // FOX_HEADS
Q_BLOCK = 128
SSM_D_INNER = 2 * D_MODEL
SSM_HEAD_DIM = 64
SSM_HEADS = SSM_D_INNER // SSM_HEAD_DIM
SSM_GROUPS = 8
SSM_HEADS_PER_GROUP = SSM_HEADS // SSM_GROUPS
SSM_STATE = 128
SSM_CONV = 4
SSM_CHUNK = 128
SSM_CONV_DIM = SSM_D_INNER + 2 * SSM_GROUPS * SSM_STATE
SSM_IN_DIM = SSM_D_INNER + SSM_CONV_DIM + SSM_HEADS
D_FF = 4 * D_MODEL
LN_EPS = 1e-5
RMS_EPS = 1e-5

kernel_name = 'hybrid_fox_ssd_sqrelu_deepnorm_adaln'

def layer_norm(x, g, b):
    xf = x.astype(jnp.float32)
    mu = jnp.mean(xf, axis=-1, keepdims=True)
    var = jnp.mean(jnp.square(xf - mu), axis=-1, keepdims=True)
    return ((xf - mu) * lax.rsqrt(var + LN_EPS) * g.astype(jnp.float32) + b.astype(jnp.float32)).astype(x.dtype)

def fox_attention(u, w_in, b_f, w_o):
    bsz, s, _ = u.shape
    h, dh = FOX_HEADS, FOX_HEAD_DIM
    proj = u @ w_in
    q, k, v, f = jnp.split(proj, [D_MODEL, 2 * D_MODEL, 3 * D_MODEL], axis=-1)
    q = q.reshape(bsz, s, h, dh).transpose(0, 2, 1, 3)
    k = k.reshape(bsz, s, h, dh).transpose(0, 2, 1, 3)
    v = v.reshape(bsz, s, h, dh).transpose(0, 2, 1, 3)
    log_f = jax.nn.log_sigmoid((f + b_f).astype(jnp.float32))
    cum = jnp.cumsum(log_f, axis=1).transpose(0, 2, 1)
    nb = s // Q_BLOCK
    q_blocks = q.reshape(bsz, h, nb, Q_BLOCK, dh).transpose(2, 0, 1, 3, 4)
    cum_blocks = cum.reshape(bsz, h, nb, Q_BLOCK).transpose(2, 0, 1, 3)
    pos_blocks = jnp.arange(s, dtype=jnp.int32).reshape(nb, Q_BLOCK)
    key_pos = jnp.arange(s, dtype=jnp.int32)
    scale = dh ** -0.5

    def block(args):
        qb, cb, pb = args
        logits = jnp.einsum('bhqd,bhkd->bhqk', qb, k).astype(jnp.float32) * scale
        logits = logits + cb[..., :, None] - cum[:, :, None, :]
        causal = pb[:, None] >= key_pos[None, :]
        logits = jnp.where(causal, logits, -jnp.inf)
        p = jax.nn.softmax(logits, axis=-1).astype(v.dtype)
        return jnp.einsum('bhqk,bhkd->bhqd', p, v)

    out = lax.map(block, (q_blocks, cum_blocks, pos_blocks))
    out = out.transpose(1, 0, 3, 2, 4).reshape(bsz, s, D_MODEL)
    return out @ w_o

def causal_depthwise_conv(x, w, b):
    kw, ch = w.shape
    y = lax.conv_general_dilated(x, w[:, None, :], window_strides=(1,), padding=[(kw - 1, 0)],
                                 dimension_numbers=('NWC', 'WIO', 'NWC'), feature_group_count=ch)
    return y + b

def ssd_mixer(u, w_in, conv_w, conv_b, dt_bias, a_log, d_skip, norm_w, w_out):
    bsz, s, _ = u.shape
    g, r, n, p, l = SSM_GROUPS, SSM_HEADS_PER_GROUP, SSM_STATE, SSM_HEAD_DIM, SSM_CHUNK
    f32 = jnp.float32
    proj = u @ w_in
    z, xbc, dt = jnp.split(proj, [SSM_D_INNER, SSM_D_INNER + SSM_CONV_DIM], axis=-1)
    xbc = jax.nn.silu(causal_depthwise_conv(xbc, conv_w, conv_b))
    xs, bm, cm = jnp.split(xbc, [SSM_D_INNER, SSM_D_INNER + g * n], axis=-1)
    nc = s // l
    xc = xs.astype(f32).reshape(bsz, nc, l, g, r, p)
    bc = bm.astype(f32).reshape(bsz, nc, l, g, n)
    cc = cm.astype(f32).reshape(bsz, nc, l, g, n)
    dt = jax.nn.softplus((dt + dt_bias).astype(f32))
    a = -jnp.exp(a_log.astype(f32))
    dt_c = dt.reshape(bsz, nc, l, g, r)
    a_cs = jnp.cumsum((dt_c * a.reshape(g, r)).transpose(0, 1, 3, 4, 2), axis=-1)
    xdt = xc * dt_c[..., None]
    cb = jnp.einsum('bclgn,bcsgn->bcgls', cc, bc)
    seg = a_cs[..., :, None] - a_cs[..., None, :]
    tril = jnp.tril(jnp.ones((l, l), dtype=bool))
    decay_in = jnp.exp(jnp.where(tril, seg, -jnp.inf))
    y_diag = jnp.einsum('bcgls,bcgrls,bcsgrp->bclgrp', cb, decay_in, xdt)
    decay_to_end = jnp.exp(a_cs[..., -1:] - a_cs)
    states = jnp.einsum('bclgn,bcgrl,bclgrp->bcgrpn', bc, decay_to_end, xdt)
    chunk_decay = jnp.exp(a_cs[..., -1])

    def step(hst, inp):
        s_c, d_c = inp
        return hst * d_c[..., None, None] + s_c, hst

    h0 = jnp.zeros_like(states[:, 0])
    _, prev = lax.scan(step, h0, (states.transpose(1, 0, 2, 3, 4, 5), chunk_decay.transpose(1, 0, 2, 3)))
    prev = prev.transpose(1, 0, 2, 3, 4, 5)
    y_off = jnp.einsum('bclgn,bcgrpn,bcgrl->bclgrp', cc, prev, jnp.exp(a_cs))
    y = y_diag + y_off + xc * d_skip.astype(f32).reshape(g, r)[:, :, None]
    y = y.reshape(bsz, s, SSM_D_INNER)
    yg = (y * jax.nn.silu(z.astype(f32))).reshape(bsz, s, g, SSM_D_INNER // g)
    yg = yg * lax.rsqrt(jnp.mean(jnp.square(yg), axis=-1, keepdims=True) + RMS_EPS)
    y = (yg.reshape(bsz, s, SSM_D_INNER) * norm_w.astype(f32)).astype(u.dtype)
    return y @ w_out

def sq_relu_mlp(u, w1, w2):
    return jnp.square(jax.nn.relu(u @ w1)) @ w2

def setup_inputs(seed: int = 0) -> dict:
    key = jax.random.key(seed)
    ks = jax.random.split(key, 24)
    n_a = (DEPTH + 1) // 2
    n_b = DEPTH // 2
    beta = (8.0 * DEPTH) ** -0.25
    f32 = jnp.float32

    def nrm(k, shape, fan_in, s=1.0):
        return jax.random.normal(k, shape, f32) * (s * fan_in ** -0.5)

    def small(k, shape, s=0.02):
        return jax.random.normal(k, shape, f32) * s

    dt0 = jnp.exp(jax.random.uniform(ks[17], (n_b, SSM_HEADS), f32, np.log(1e-3), np.log(1e-1)))
    dt_bias = dt0 + jnp.log(-jnp.expm1(-dt0))
    a_log = jnp.log(jax.random.uniform(ks[18], (n_b, SSM_HEADS), f32, 1.0, 16.0))
    return {
        'x': jax.random.normal(ks[0], (BATCH, SEQ, D_MODEL), f32),
        'c': jax.random.normal(ks[1], (BATCH, D_MODEL), f32),
        'ada_w': nrm(ks[2], (DEPTH, D_MODEL, 6 * D_MODEL), D_MODEL, 0.1),
        'ada_b': small(ks[3], (DEPTH, 6 * D_MODEL), 0.01),
        'ln_mix_g': 1.0 + small(ks[4], (DEPTH, D_MODEL)),
        'ln_mix_b': small(ks[5], (DEPTH, D_MODEL)),
        'ln_mlp_g': 1.0 + small(ks[6], (DEPTH, D_MODEL)),
        'ln_mlp_b': small(ks[7], (DEPTH, D_MODEL)),
        'mlp_w1': nrm(ks[8], (DEPTH, D_MODEL, D_FF), D_MODEL),
        'mlp_w2': nrm(ks[9], (DEPTH, D_FF, D_MODEL), D_FF, beta),
        'fox_w_in': nrm(ks[10], (n_a, D_MODEL, 3 * D_MODEL + FOX_HEADS), D_MODEL),
        'fox_b_f': 2.0 + small(ks[11], (n_a, FOX_HEADS), 0.1),
        'fox_w_o': nrm(ks[12], (n_a, D_MODEL, D_MODEL), D_MODEL, beta),
        'ssm_w_in': nrm(ks[13], (n_b, D_MODEL, SSM_IN_DIM), D_MODEL),
        'ssm_conv_w': nrm(ks[14], (n_b, SSM_CONV, SSM_CONV_DIM), SSM_CONV),
        'ssm_conv_b': small(ks[15], (n_b, SSM_CONV_DIM)),
        'ssm_dt_bias': dt_bias,
        'ssm_a_log': a_log,
        'ssm_d': 1.0 + small(ks[16], (n_b, SSM_HEADS)),
        'ssm_norm_w': 1.0 + small(ks[19], (n_b, SSM_D_INNER)),
        'ssm_w_out': nrm(ks[20], (n_b, SSM_D_INNER, D_MODEL), SSM_D_INNER, beta),
    }

def reference(x, c, ada_w, ada_b, ln_mix_g, ln_mix_b, ln_mlp_g, ln_mlp_b, mlp_w1, mlp_w2,
              fox_w_in, fox_b_f, fox_w_o, ssm_w_in, ssm_conv_w, ssm_conv_b, ssm_dt_bias,
              ssm_a_log, ssm_d, ssm_norm_w, ssm_w_out):
    alpha = (2.0 * DEPTH) ** 0.25
    cond = jax.nn.silu(c)
    for i in range(DEPTH):
        mod = (cond @ ada_w[i] + ada_b[i])[:, None, :]
        sh_a, sc_a, g_a, sh_m, sc_m, g_m = jnp.split(mod, 6, axis=-1)
        u = x * (1.0 + sc_a) + sh_a
        j = i // N_MIXERS
        if i % N_MIXERS == 0:
            y = fox_attention(u, fox_w_in[j], fox_b_f[j], fox_w_o[j])
        else:
            y = ssd_mixer(u, ssm_w_in[j], ssm_conv_w[j], ssm_conv_b[j], ssm_dt_bias[j],
                          ssm_a_log[j], ssm_d[j], ssm_norm_w[j], ssm_w_out[j])
        x = layer_norm(alpha * x + (1.0 + g_a) * y, ln_mix_g[i], ln_mix_b[i])
        u = x * (1.0 + sc_m) + sh_m
        y = sq_relu_mlp(u, mlp_w1[i], mlp_w2[i])
        x = layer_norm(alpha * x + (1.0 + g_m) * y, ln_mlp_g[i], ln_mlp_b[i])
    return x


_drawn_inputs = setup_inputs


def setup_inputs(seed=0):
    import zlib

    import numpy as np

    out = dict(_drawn_inputs(seed))
    spreads = {}
    factors = {'ada_b': 3.74, 'fox_b_f': 5.192, 'ssm_conv_b': 5.975, 'ssm_d': 8.0, 'ssm_norm_w': 8.0}
    for name, (base, spread) in spreads.items():
        noise = np.random.default_rng([zlib.crc32(name.encode()), seed]).standard_normal(out[name].shape)
        drawn = base * np.exp(spread * noise) if base else spread * noise
        out[name] = __import__('jax').numpy.asarray(drawn.astype(out[name].dtype))
    for name, factor in factors.items():
        out[name] = (out[name] * factor).astype(out[name].dtype)
    return out
```

```python
import numpy as np

import concourse.bass as bass
from concourse import mybir

F32 = mybir.dt.float32
F32R = mybir.dt.float32r
ALU = mybir.AluOpType
ACT = mybir.ActivationFunctionType
AX = mybir.AxisListType
ds = bass.ds

P128 = 128
D = 1024
S = 1024
KT = D // P128
HALF = 512
FF = 4 * D
HEADS, DH = 16, 64
PAIRS = HEADS // 2
QB = S // P128
DI = 2 * D
GROUPS = 8
NSTATE = 128
HPG = 4
DT0 = DI + DI + 2 * GROUPS * NSTATE
MASKED = -(2.0 ** 100)
EPS = 1e-5
ALPHA = (2.0 * 2) ** 0.25

P_FOX = 1
P_WO = P_FOX + 3 * PAIRS
P_MLP0 = P_WO + KT
P_DT = P_MLP0 + 64
P_SSM = P_DT + 1
P_OUT = P_SSM + 6 * GROUPS
P_MLP1 = P_OUT + 2 * KT
P_END = P_MLP1 + 64
U_F = 8
U_FOX = U_F + 1
U_WO = U_FOX + 4 * PAIRS
U_OF_P = U_WO - P_WO
U_END = P_END + U_OF_P
ADA_JOBS = 80


class Count:

    def __init__(self, sem):
        self.sem, self.base, self.k = sem, 0, 0

    @property
    def n(self):
        return self.base + self.k

    def at(self, base):
        self.base, self.k = base, 0

    def inc(self, ins):
        ins.then_inc(self.sem, 1)
        self.k += 1


def rounds(eng, work):
    work(0, 0, True, False)
    with eng.Fori(0, 3) as r:
        work(2 * r + 1, 1, True, True)
        work(2 * r + 2, 0, True, True)
    work(7, 1, True, True)
    work(8, 0, False, True)


def build(nc, x, c, ada_w, ada_b, ln_mix_g, ln_mix_b, ln_mlp_g, ln_mlp_b, mlp_w1, mlp_w2,
          fox_w_in, fox_b_f, fox_w_o, ssm_w_in, ssm_conv_w, ssm_conv_b, ssm_dt_bias,
          ssm_a_log, ssm_d, ssm_norm_w, ssm_w_out, out):
    base = (nc.sbuf_base + 31) // 32 * 32
    top = [base]

    def place(name, shape, dt, off):
        return nc.alloc_sbuf_tensor_at(name, shape, dt, offset=off)

    def keep(name, shape, dt=F32):
        off = top[0]
        top[0] += (int(np.prod(shape[1:])) * 4 + 31) // 32 * 32
        return place(name, shape, dt, off)

    UH, UL = keep("UH", [128, KT, S], F32R), keep("UL", [128, KT, S], F32R)
    RAW = keep("RAW", [128, 2, KT, 128])
    WH, WL = keep("WH", [128, 2, KT, 128], F32R), keep("WL", [128, 2, KT, 128], F32R)
    ADARAW, ADAACC = keep("ADARAW", [128, KT, 128]), keep("ADAACC", [128, 2, 128])
    IDF, IDR = keep("IDF", [128, 128]), keep("IDR", [128, 128], F32R)
    ONESF = keep("ONESF", [128, 128])
    MASKA = keep("MASKA", [128, 128], F32R)
    ONES2 = keep("ONES2", [128, 128], F32R)
    VEC1, VEC2, VEC3 = keep("VEC1", [128, 104]), keep("VEC2", [128, 112]), keep("VEC3", [128, 128])
    MOD = keep("MOD", [128, 96])
    COND = keep("COND", [128, 16])
    COLS = keep("COLS", [128, 4, 4, 8])
    G1 = keep("G1", [128, 4, 8])
    CBH = keep("CBH", [128, 32])
    DCOL = keep("DCOL", [128, 16])
    DALL = keep("DALL", [128, 32])
    SMALL = keep("SMALL", [128, 16])
    NEGM, RSUM, RINV = keep("NEGM", [128, 8]), keep("RSUM", [128, 8]), keep("RINV", [128, 8])
    W0 = top[0]
    K = 1024

    def at(name, shape, kb, dt=F32):
        return place(name, shape, dt, W0 + int(kb * K))

    HH, HL = at("HH", [128, KT, S], 0, F32R), at("HL", [128, KT, S], 32, F32R)
    Y0, Y1 = at("Y0", [128, KT, S], 0), at("Y1", [128, KT, S], 32)
    R = at("R", [128, KT, S], 64)
    TA, TB, SQ = at("TA", [128, S], 96), at("TB", [128, S], 100), at("SQ", [128, HALF], 104)
    LA, LB, LM = at("LA", [128, S], 0), at("LB", [128, S], 4), at("LM", [128, S], 12)
    U32 = at("U32", [128, 2, HALF], 8)
    LV, LS = at("LV", [128, S], 16), at("LS", [128, S], 20)
    XIN = at("XIN", [128, KT, D], 0)
    ADA0 = at("ADA0", [128, KT, 2 * D], 32)
    RST = at("RST", [128, 2, S], 96)
    XU = at("XU", [128, 2, S], 32)
    VIN = at("VIN", [128, 3, 128], 104)
    QH, QL = at("QH", [128, 2, S], 32, F32R), at("QL", [128, 2, S], 40, F32R)
    KH, KL = at("KH", [128, 2, S], 48, F32R), at("KL", [128, 2, S], 56, F32R)
    VH, VL = at("VH", [128, 2, QB, 128], 64, F32R), at("VL", [128, 2, QB, 128], 72, F32R)
    VT = at("VT", [128, S], 80)
    PE_ = at("PEXP", [128, S], 84)
    PH, PL = at("PH", [128, S], 88, F32R), at("PL", [128, S], 92, F32R)
    PTH, PTL = at("PTH", [128, QB, 128], 96, F32R), at("PTL", [128, QB, 128], 100, F32R)
    NCR = at("NCR", [128, S], 104, F32R)
    FZ, FM, FE, FU = (at(n, [128, S], 84 + 4 * i) for i, n in enumerate(("FZ", "FM", "FE", "FU")))
    FL, FC = at("FL", [128, S], 100), at("FC", [128, S], 80)
    FNH, FNL = at("FNH", [128, S], 36, F32R), at("FNL", [128, S], 44, F32R)
    OST = at("OST", [128, 2, D], 24)
    XS = [at("XS0", [128, 2, S], 0), at("XS1", [128, 2, S], 48)]
    BC = [at("BC0", [128, 2, S], 8), at("BC1", [128, 2, S], 56)]
    XP = at("XP", [128, 3 + S + 1], 16)
    CT, TT = at("CT", [128, S], 20.25), at("TT", [128, S], 24.25)
    YR = at("YR", [128, 2, 2, S], 32)
    ES, MS, CS = at("ES", [128, HPG, 128], 64), at("MS", [128, HPG, 128], 66), at("CS", [128, HPG, 128], 68)
    XD, XE = at("XD", [128, 256], 70), at("XE", [128, 256], 71)
    BT = at("BT", [128, 128], 72)
    HS, HT = at("HS", [128, 256], 73), at("HT", [128, 256], 74)
    AROW = at("AROW", [128, S], 75, F32R)
    SEL = at("SEL", [128, 8, 128], 79, F32R)
    MASKS = at("MASKS", [128, HPG, 128], 83, F32R)
    TDT, TAC, TDE = (at(n, [128, QB, 32], 85 + i) for i, n in enumerate(("TDT", "TAC", "TDE")))
    SQ2, RS2 = at("SQ2", [128, S], 88), at("RS2", [128, S], 92)
    SELF, MASKF = at("SELF", [128, 8, 128], 96), at("MASKF", [128, HPG, 128], 100)
    DZ, DE, DU, DL = (at(n, [128, S], 48 + 4 * i) for i, n in enumerate(("DZ", "DE", "DU", "DL")))
    DTT, ACS, EAC, DDE = (at(n, [128, S], kb) for n, kb in (("DTT", 88), ("ACS", 92), ("EAC", 96), ("DDE", 100)))
    RWH = [at("RWH0", [128, S], 40, F32R), at("RWH1", [128, S], 64, F32R)]
    RWL = [at("RWL0", [128, S], 44, F32R), at("RWL1", [128, S], 68, F32R)]
    assert W0 + 108 * K <= nc.sbuf_usable_end, (W0, nc.sbuf_usable_end)

    XSCR = nc.dram_tensor("xscr", (2, KT, 128, S), F32).ap()
    CSCR = nc.dram_tensor("cscr", (HEADS, 2, S), F32).ap()
    ASCR = nc.dram_tensor("ascr", (4, GROUPS * HPG, S), F32).ap()
    YSCR = nc.dram_tensor("yscr", (2 * KT, 128, S), F32).ap()

    PS = nc.alloc_psum_tensor("PS", [128, 8 * HALF], F32)

    def bank(b, n=1):
        return PS[:, b * HALF:(b + n) * HALF]

    def pp(slot):
        return bank(2 * slot, 2)

    SEM = {}

    def sem(name):
        if name not in SEM:
            SEM[name] = nc.alloc_semaphore(name)
        return SEM[name]

    raw_in = [sem("raw_in0"), sem("raw_in1")]
    w_split = sem("w_split")
    pp_full = sem("pp_full")
    pp_free = sem("pp_free")
    xsp0 = [sem("xspill0_even"), sem("xspill0_odd")]
    ada_in, ada_done, ada_ps, ada_ev = sem("ada_in"), sem("ada_done"), sem("ada_ps"), sem("ada_ev")
    w_pan = [w.rearrange("(k p) n -> p k n", p=128) for w in (fox_w_in[0], fox_w_o[0], ssm_w_in[0], ssm_w_out[0])]
    FOXW, WOW, SSMW, SOUTW = w_pan
    W1W = [mlp_w1[i].rearrange("(k p) n -> p k n", p=128) for i in range(2)]
    W2W = [mlp_w2[i].rearrange("(k p) n -> p k n", p=128) for i in range(2)]
    ADAW = [ada_w[i].rearrange("(k p) n -> p k n", p=128) for i in range(2)]

    with nc.Block() as block:
        @block.sync
        def _(sp):
            sp.dma_start(VIN[0:96, 0, :], ada_b.rearrange("l (r q) -> (l r) q", q=128)).then_inc(sem("vin"), 16)
            sp.dma_start(VIN[96:104, 0, :], c.rearrange("a (r q) -> (a r) q", q=128)).then_inc(sem("vin"), 16)
            for n, v in enumerate((ln_mix_g, ln_mix_b, ln_mlp_g, ln_mlp_b)):
                sp.dma_start(VIN[16 * n:16 * n + 16, 1, :], v.rearrange("l (r q) -> (l r) q", q=128)).then_inc(sem("vin"), 16)
            sp.dma_start(VIN[64:96, 1, :], ssm_conv_b.rearrange("a (r q) -> (a r) q", q=128)).then_inc(sem("vin"), 16)
            sp.dma_start(VIN[96:112, 1, :], ssm_norm_w.rearrange("a (r q) -> (a r) q", q=128)).then_inc(sem("vin"), 16)
            sp.dma_start(VIN[:, 2, :], ssm_conv_w[0].rearrange("t (r q) -> (t r) q", q=128)).then_inc(sem("vin"), 16)
            for k in range(KT):
                sp.dma_start(ADA0[:, k, :], ADAW[0][:, k, 0:2 * D]).then_inc(sem(f"ada0_{k}"), 16)
            xt = x[0].rearrange("(t p) d -> p t d", p=128)
            for h in range(2):
                sp.dma_start(XIN[:, 4 * h:4 * h + 4, :], xt[:, 4 * h:4 * h + 4, :]).then_inc(sem(f"xin{h}"), 16)
            sp.dma_start(DALL[:], ssm_d[0:1, :].partition_broadcast(128).rearrange("p a n -> p (a n)")).then_inc(sem("small_in"), 16)
            sp.wait_ge(sem("small_z"), 1)
            sp.dma_start(SMALL[112:128, 0:1], fox_b_f.rearrange("a h -> h a")).then_inc(sem("small_in"), 16)
            sp.dma_start(SMALL[96:128, 1:2], ssm_dt_bias.rearrange("a h -> h a")).then_inc(sem("small_in"), 16)
            sp.dma_start(SMALL[96:128, 2:3], ssm_a_log.rearrange("a h -> h a")).then_inc(sem("small_in"), 16)

            def load(P, par, src):
                if not (isinstance(P, int) and P < 2):
                    sp.wait_ge(w_split, P - 1)
                    sp.sem_inc(sem("load_go"), 1)
                sp.dma_start(RAW[:, par], src).then_inc(raw_in[par], 16)

            def load_ada(n, layer, col):
                if not (isinstance(n, int) and n == 0):
                    sp.wait_ge(ada_done, n)
                sp.dma_start(ADARAW[:], ADAW[layer][:, :, ds(col, 128)]).then_inc(ada_in, 16)

            load(0, 0, FOXW[:, :, 3 * D + HEADS - 128:3 * D + HEADS])
            for j in range(3):
                load(1 + j, (1 + j) % 2, FOXW[:, :, j * D:j * D + 128])
                load_ada(j, 0, (16 + j) * 128)
            for j in range(3):
                load(4 + j, j % 2, FOXW[:, :, j * D + 128:j * D + 256])
                load_ada(3 + j, 0, (19 + j) * 128)
            with sp.Fori(0, 3) as r:
                for k in range(6):
                    load(7 + 6 * r + k, (7 + k) % 2, FOXW[:, :, ds(256 * r + (k % 3) * D + (2 + k // 3) * 128, 128)])
                    load_ada(6 + 6 * r + k, 0, 768 * r + (22 + k) * 128)
            with sp.Fori(0, KT // 2) as r:
                for k in range(2):
                    load(P_WO + 2 * r + k, (P_WO + k) % 2, WOW[:, :, ds(256 * r + k * 128, 128)])
                    load_ada(24 + 2 * r + k, 0, 256 * r + (40 + k) * 128)

            def mlp(layer, P0, groups, ada):
                with sp.Fori(0, groups) as f:
                    with sp.Fori(0, KT // 2) as r:
                        for k in range(2):
                            load(P0 + 16 * f + 2 * r + k, (P0 + k) % 2, W1W[layer][:, :, ds(1024 * f + 256 * r + 128 * k, 128)])
                            if ada:
                                load_ada(32 + 16 * f + 2 * r + k, 1, 2048 * f + 256 * r + k * 128)
                    with sp.Fori(0, KT // 2) as r:
                        for k in range(2):
                            load(P0 + 16 * f + 8 + 2 * r + k, (P0 + k) % 2, W2W[layer][:, ds(8 * f, 8), ds(256 * r + 128 * k, 128)])
                            if ada:
                                load_ada(40 + 16 * f + 2 * r + k, 1, 2048 * f + 1024 + 256 * r + k * 128)

            def mlp_last(layer, P0):
                for st, (w, k0) in enumerate(((W1W[layer], 0), (W2W[layer], 24))):
                    with sp.Fori(0, KT // 2) as r:
                        for k in range(2):
                            col = 256 * r + 128 * k + (3072 if st == 0 else 0)
                            load(P0 + 48 + 8 * st + 2 * r + k, (P0 + k) % 2, w[:, k0:k0 + 8, ds(col, 128)])

            mlp(0, P_MLP0, 3, True)
            mlp_last(0, P_MLP0)
            load(P_DT, P_DT % 2, SSMW[:, :, DT0 + 32 - 128:DT0 + 32])
            with sp.Fori(0, GROUPS) as g:
                for j, (c0, step) in enumerate(((2 * DI, 128), (2 * DI + D, 128), (DI, 256), (DI + 128, 256), (0, 256), (128, 256))):
                    load(P_SSM + 6 * g + j, (P_SSM + j) % 2, SSMW[:, :, ds(step * g + c0, 128)])
            with sp.Fori(0, 2) as f:
                with sp.Fori(0, KT // 2) as r:
                    for k in range(2):
                        load(P_OUT + 8 * f + 2 * r + k, (P_OUT + k) % 2, SOUTW[:, ds(8 * f, 8), ds(256 * r + 128 * k, 128)])
            mlp(1, P_MLP1, 3, False)
            mlp_last(1, P_MLP1)

        @block.gpsimd
        def _(pool):
            ch = Count(sem("pool_c"))

            def do(ins):
                ch.inc(ins)
                pool.wait_ge(ch.sem, ch.n)

            do(pool.memset(IDF[:], 0.0))
            do(pool.affine_select(out=IDF[:], in_=IDF[:], compare_op=ALU.not_equal, fill=1.0, base=0,
                                  pattern=[[-1, 128]], channel_multiplier=1))
            pool.memset(ONESF[:], 1.0).then_inc(sem("consts"), 1)
            do(pool.tensor_scalar(IDR[:], IDF[:], 1.0, 1.0, ALU.mult, ALU.mult))
            do(pool.memset(ADAACC[:, 0, :], 0.0))
            do(pool.affine_select(out=ADAACC[:, 0, :], in_=ADAACC[:, 0, :], compare_op=ALU.is_ge, fill=MASKED, base=0,
                                  pattern=[[-1, 128]], channel_multiplier=1))
            do(pool.tensor_scalar(MASKA[:], ADAACC[:, 0, :], 1.0, 1.0, ALU.mult, ALU.mult))
            do(pool.memset(ONES2[:].bitcast(F32), 0.0))
            do(pool.memset(ONES2[0:2, :].bitcast(F32), 1.0))
            do(pool.memset(ONES2[64:66, :].bitcast(F32), 1.0))
            pool.wait_ge(sem("vec_ps"), 1)
            pool.memset(NCR[:].bitcast(F32), 0.0).then_inc(sem("consts"), 1)
            pool.sem_inc(sem("whi"), 1)

            def split(P, par, used):
                pool.wait_ge(raw_in[par], 16 * ((P - par) // 2 + 1) if isinstance(P, int) else used[1])
                if used[0] is not None:
                    pool.wait_ge(pp_full, used[0])
                pool.sem_inc(sem("split_go"), 1)
                pool.tensor_scalar(WH[:, par], RAW[:, par], 1.0, 1.0, ALU.mult, ALU.mult).then_inc(sem("whi"), 1)
                pool.wait_ge(sem("whi"), P + 2)
                pool.tensor_tensor(WL[:, par], RAW[:, par], WH[:, par].bitcast(F32), ALU.subtract).then_inc(w_split, 1)

            def panel(P, par, U2):
                split(P, par, (U2, 8 * P + (16 - 8 * par)))

            cond = COND[:, 0:8].unsqueeze(2).broadcast_to([128, KT, 128])

            def ada(n, slot):
                pool.wait_ge(ada_in, 16 * n + 16)
                pool.wait_ge(ada_ev, n + 1)
                s = sem("ada_c")
                v = ADARAW[:]
                steps = [lambda: pool.tensor_tensor(v, v, cond, ALU.mult),
                         lambda: pool.tensor_tensor(v[:, 0:4], v[:, 0:4], v[:, 4:8], ALU.add),
                         lambda: pool.tensor_tensor(v[:, 0:2], v[:, 0:2], v[:, 2:4], ALU.add)]
                for i, f in enumerate(steps):
                    f().then_inc(s, 1)
                    pool.wait_ge(s, 3 * n + i + 1)
                pool.tensor_tensor(ADAACC[:, slot], v[:, 0], v[:, 1], ALU.add).then_inc(ada_done, 1)

            panel(0, 0, None)
            panel(1, 1, None)
            pool.wait_ge(sem("cond"), 1)
            ada(0, 0)
            panel(2, 0, U_F + 1)
            ada(1, 1)
            with pool.Fori(0, 4) as r:
                r8 = 8 * r
                for k in range(6):
                    panel(6 * r + (3 + k), (3 + k) % 2, r8 + (U_FOX + 4 * (k // 3) + k % 3 + 1))
                    ada(6 * r + (2 + k), k % 2)

            def to_u(m, src):
                pool.tensor_scalar(UH[:, m], src[:, m], 1.0, 1.0, ALU.mult, ALU.mult).then_inc(sem("uhp"), 1)

            pool.wait_ge(pp_full, U_WO - 1)
            for m in range(KT):
                pool.wait_ge(sem("pv_ev"), 4 * (m + 1) + 1)
                to_u(m, Y0)
                pool.wait_ge(sem("uhp"), m + 1)
                pool.tensor_tensor(UL[:, m], Y0[:, m], UH[:, m].bitcast(F32), ALU.subtract).then_inc(sem("ulp"), 1)
            with pool.Fori(0, (P_MLP0 + 48 - 27) // 2) as r:
                for k in range(2):
                    panel(2 * r + (27 + k), (27 + k) % 2, 2 * r + (25 + k + U_OF_P + 1))
                    ada(2 * r + (26 + k), k % 2)
            with pool.Fori(0, (P_DT + 2 - (P_MLP0 + 48)) // 2) as r:
                for k in range(2):
                    P = P_MLP0 + 48 + k
                    panel(2 * r + P, P % 2, 2 * r + (P - 2 + U_OF_P + 1))
            ch2 = Count(sem("pool_c2"))

            def do2(ins):
                ch2.inc(ins)
                pool.wait_ge(ch2.sem, ch2.n)

            pool.wait_ge(sem("xspill1"), 16 * KT)
            do2(pool.memset(SELF[:], 0.0))
            sv = SELF[:].rearrange("p (a h) n -> p a h n", a=2)
            for b in (0, -4):
                do2(pool.affine_select(out=sv, in_=sv, compare_op=ALU.not_equal, fill=1.0, base=b,
                                       pattern=[[-8, 2], [-1, 4], [0, 128]], channel_multiplier=1))
            do2(pool.tensor_scalar(SEL[:], SELF[:], 1.0, 1.0, ALU.mult, ALU.mult))
            do2(pool.memset(MASKF[:], 0.0))
            do2(pool.affine_select(out=MASKF[:], in_=MASKF[:], compare_op=ALU.is_ge, fill=MASKED, base=0,
                                   pattern=[[0, 4], [1, 128]], channel_multiplier=-1))
            do2(pool.tensor_scalar(MASKS[:], MASKF[:], 1.0, 1.0, ALU.mult, ALU.mult))
            pool.memset(AROW[:].bitcast(F32), 0.0).then_inc(sem("ssm_consts"), 1)
            panel(P_SSM + 1, (P_SSM + 1) % 2, P_SSM - 1 + U_OF_P + 1)
            with pool.Fori(0, GROUPS * 3) as r:
                for k in range(2):
                    P = P_SSM + 2 + k
                    panel(2 * r + P, P % 2, 2 * r + (P - 2 + U_OF_P + 1))
            for m in range(KT):
                pool.wait_ge(sem(f"y0_in{m}"), 16)
                to_u(m, Y0)
                pool.wait_ge(sem("uhp"), KT + m + 1)
                pool.tensor_tensor(UL[:, m], Y0[:, m], UH[:, m].bitcast(F32), ALU.subtract).then_inc(sem("ulp"), 1)
            for m in range(KT):
                if m < 6:
                    P = P_OUT + 2 + m
                    panel(P, P % 2, P - 2 + U_OF_P + 1)
                pool.wait_ge(sem(f"y1_in{m}"), 16)
                pool.wait_ge(sem("ulp"), 2 * KT)
                pool.tensor_scalar(HH[:, m], Y1[:, m], 1.0, 1.0, ALU.mult, ALU.mult).then_inc(sem("hhp"), 1)
                pool.wait_ge(sem("hhp"), m + 1)
                pool.tensor_tensor(HL[:, m], Y1[:, m], HH[:, m].bitcast(F32), ALU.subtract).then_inc(sem("hlp"), 1)
            end = P_END
            with pool.Fori(0, (end - (P_OUT + 8)) // 2) as r:
                for k in range(2):
                    P = P_OUT + 8 + k
                    panel(2 * r + P, P % 2, 2 * r + (P - 2 + U_OF_P + 1))

        @block.tensor
        def _(pe):
            def panel(slot, par, xh, xl, lo=0, hi=48, wait_k=None, wait_h=None):
                P_ = pp(slot)
                if wait_h is not None:
                    for h in range(2):
                        for k in range(KT):
                            wait_h(h, k)
                            v = slice(h * HALF, (h + 1) * HALF)
                            for j, (w, m) in enumerate(((WH, xh), (WH, xl), (WL, xh))):
                                mm = pe.matmul(P_[:, v], w[:, par, k, :], m[:, k, v], start=(k == 0 and j == 0),
                                               stop=(k == KT - 1 and j == 2))
                    return mm
                for n in range(lo, hi):
                    k, j = divmod(n, 6)
                    if j == 0 and wait_k is not None:
                        wait_k(k)
                    w, v, h = ((WH, xh, 0), (WH, xh, 1), (WH, xl, 0), (WH, xl, 1), (WL, xh, 0), (WL, xh, 1))[j]
                    mm = pe.matmul(P_[:, h * HALF:(h + 1) * HALF], w[:, par, k, :], v[:, k, h * HALF:(h + 1) * HALF],
                                   start=(k == 0 and j < 2), stop=(k == KT - 1 and j >= 4))
                return mm

            def begin(P, U, ahead=1):
                pe.wait_ge(w_split, P + 1)
                pe.wait_ge(pp_free, U + ahead)

            def ada(n, slot):
                pe.wait_ge(ada_done, n + 1)
                pe.wait_ge(ada_ev, n + 2)
                pe.matmul(bank(7)[:, 0:1], ADAACC[:, slot], ONESF[:, 0:1], start=True, stop=True).then_inc(ada_ps, 1)

            pe.wait_ge(sem("pool_c"), 2)
            pe.wait_ge(sem("vin"), 16 * 9)
            for n, rows in enumerate((104, 112, 128)):
                mm = pe.transpose(bank(4)[:, 128 * n:128 * n + rows], VIN[0:rows, n, :], IDF[0:rows, 0:rows])
            mm.then_inc(sem("vec_ps"), 1)
            pe.wait_ge(sem("cond"), 1)
            for k in range(KT):
                pe.wait_ge(sem(f"ada0_{k}"), 16)
                for j in range(16):
                    mm = pe.matmul(bank(5)[:, j:j + 1], ADA0[:, k, j * 128:(j + 1) * 128], COND[:, k:k + 1],
                                   start=(k == 0 and j == 0), stop=(k == KT - 1), skip_group_check=True)
            mm.then_inc(sem("ada0_ps"), 1)
            pe.wait_ge(sem("xin0"), 16)
            pe.wait_ge(sem("xin1"), 16)
            for k in range(KT):
                pe.wait_ge(pp_free, k + 1)
                for t in range(QB):
                    mm = pe.transpose(pp(k % 2)[:, t * 128:(t + 1) * 128], XIN[:, t, k * 128:(k + 1) * 128], IDF[:])
                mm.then_inc(pp_full, 1)
            begin(0, U_F)
            panel(0, 0, UH, UL, wait_k=lambda k: pe.wait_ge(sem("ul"), k + 1)).then_inc(pp_full, 1)

            def fox(it, par, panels, attend):
                a = it - 1
                pb, ab = par, 1 - par
                p0 = 1 + par
                u0 = 4 * it + U_FOX

                def filler(n):
                    j, i = divmod(n, 12)
                    if not panels or i == 11:
                        return
                    lo, hi = 48 * i // 11, 48 * (i + 1) // 11
                    if i == 0:
                        begin(3 * it + (P_FOX + j), u0 + j, 2)
                    mm = panel(0, (p0 + j) % 2, UH, UL, lo, hi)
                    if hi == 48:
                        mm.then_inc(pp_full, 1)
                        ada(3 * it + j, (par + j) % 2)

                def scores(t):
                    s, i = divmod(t, QB)
                    rows = slice(64 * s, 64 * s + 64)
                    n = 128 * (i + 1)
                    pe.wait_ge(sem("exp"), 16 * a + (t + 1))
                    for lo in range(0, n, HALF):
                        w = min(HALF, n - lo)
                        o = bank(2, 2)[:, lo:lo + w]
                        q, kk = slice(128 * i, 128 * i + 128), slice(lo, lo + w)
                        diag = lo + w == n
                        pe.matmul(o, QH[rows, ab, q], KH[rows, ab, kk], start=True, stop=False)
                        pe.matmul(o, QH[rows, ab, q], KL[rows, ab, kk], start=False, stop=False)
                        pe.matmul(o, QL[rows, ab, q], KH[rows, ab, kk], start=False, stop=False)
                        if diag:
                            pe.matmul(bank(2, 2)[:, n - 128:n], IDR[:], MASKA[:], start=False, stop=False, skip_group_check=True)
                        mm = pe.matmul(o, ONES2[rows, :], NCR[rows, kk], start=False, stop=True)
                    mm.then_inc(sem("sc"), 1)

                def turn(t, b):
                    s, i = divmod(t, QB)
                    u = 12 * s + [0, 1, 2, 3, 4, 6, 8, 10][i] + b
                    if b == 0:
                        pe.wait_ge(sem("p"), 16 * a + (t + 2))
                    pe.wait_ge(sem("pth"), 24 * a + (u + 1))
                    pe.wait_ge(sem("ptl"), 24 * a + (u + 1))
                    for part, src in ((0, PH), (1, PL)):
                        for j in range(4 * b, min(4 * b + 4, i + 1)):
                            o = bank(4 + part)[:, 128 * (j % 4):128 * (j % 4) + 128]
                            mm = pe.matmul(o, src[:, 128 * j:128 * j + 128], IDR[:], start=True, stop=True)
                    mm.then_inc(sem("pt"), 1)

                def pv(t):
                    s, i = divmod(t, QB)
                    u = 12 * s + [0, 1, 2, 3, 4, 6, 8, 10][i] + (i >= 4)
                    pe.wait_ge(sem("pth"), 24 * a + (u + 2))
                    pe.wait_ge(sem("ptl"), 24 * a + (u + 2))
                    if i % 4 == 0:
                        pe.wait_ge(sem("pv_ev"), 4 * a + (t // 4 + 1))
                    o = bank(6)[:, 128 * (i % 4):128 * (i % 4) + 128]
                    for j in range(i + 1):
                        pe.matmul(o, VH[:, ab, j], PTH[:, j], start=(j == 0), stop=False)
                        pe.matmul(o, VH[:, ab, j], PTL[:, j], start=False, stop=False)
                        mm = pe.matmul(o, VL[:, ab, j], PTH[:, j], start=False, stop=(j == i))
                    mm.then_inc(sem("pv"), 1)

                if attend:
                    pe.wait_ge(sem("ncr_in"), 32 * a + 32)
                    pe.wait_ge(pp_free, 4 * a + (U_FOX + 6))
                for t in range(18):
                    if attend:
                        if t < 16:
                            scores(t)
                        if t >= 2:
                            pv(t - 2)
                        if 1 <= t <= 16:
                            turn(t - 1, 0)
                    filler(2 * t)
                    if attend and 1 <= t <= 16 and (t - 1) % QB >= 4:
                        turn(t - 1, 1)
                    filler(2 * t + 1)
                if panels:
                    pe.wait_ge(pp_free, u0 + (3 + 2))
                    for j in range(QB):
                        mm = pe.transpose(pp(0)[:, 128 * j:128 * j + 128], VT[:, 128 * j:128 * j + 128], IDF[:])
                    mm.then_inc(pp_full, 1)

            rounds(pe, fox)

            def stats(n):
                pe.wait_ge(sem("sqd"), 14 * (n + 1))
                for q, v in enumerate((TA, TB)):
                    for h in range(2):
                        mm = pe.matmul(bank(4 + 2 * q + h), ONESF[:], v[:, h * HALF:(h + 1) * HALF], start=True, stop=True)
                mm.then_inc(sem("stats"), 1)

            with pe.Fori(0, KT // 2) as r:
                for k in range(2):
                    P = P_WO + k
                    begin(2 * r + P, 2 * r + (P + U_OF_P), 1)
                    panel((P + U_OF_P) % 2, P % 2, UH, UL, wait_k=(lambda i: pe.wait_ge(sem("ulp"), i + 1)) if k == 0 else None).then_inc(pp_full, 1)
                    ada(2 * r + (24 + k), k % 2)
            pe.wait_ge(ada_ev, 32 + 2)
            stats(0)

            def mlp(layer, P0, ul0):
                def one(off, expr, k, xh, xl, ada_too, wait_k=None, wait_h=None):
                    P = P0 + off + k
                    begin(expr + P, expr + (P + U_OF_P), 1)
                    panel((P + U_OF_P) % 2, P % 2, xh, xl, wait_k=wait_k, wait_h=wait_h).then_inc(pp_full, 1)
                    if ada_too:
                        ada(expr + (32 + off + k), k)

                def first(ada_too, f):
                    for k in range(2):
                        one(0, 0, k, UH, UL, ada_too, wait_h=lambda h, i: pe.wait_ge(sem("ul"), ul0 + 8 * h + i + 1))
                    with pe.Fori(0, KT // 2 - 1) as r:
                        for k in range(2):
                            one(2, 2 * r, k, UH, UL, ada_too)

                def second(ada_too, f):
                    with pe.Fori(0, KT // 2) as r:
                        for k in range(2):
                            one(8, 16 * f + 2 * r, k, HH, HL, ada_too,
                                wait_k=(lambda i: pe.wait_ge(sem("hl"), 8 * f + (32 * layer + i + 3))) if k == 0 else None)

                ada_too = layer == 0
                first(ada_too, 0)
                second(ada_too, 0)
                with pe.Fori(1, 3) as f:
                    with pe.Fori(0, KT // 2) as r:
                        for k in range(2):
                            one(0, 16 * f + 2 * r, k, UH, UL, ada_too)
                    second(ada_too, f)
                with pe.Fori(0, KT // 2) as r:
                    for k in range(2):
                        one(48, 2 * r, k, UH, UL, False)
                second(False, 3)

            mlp(0, P_MLP0, 8)
            pe.wait_ge(ada_ev, ADA_JOBS + 2)
            stats(1)
            begin(P_DT, P_DT + U_OF_P)
            panel((P_DT + U_OF_P) % 2, P_DT % 2, UH, UL,
                  wait_h=lambda h, k: pe.wait_ge(sem("ul"), 24 + 8 * h + k + 1)).then_inc(pp_full, 1)

            def ssm(it, par, panels, scan):
                g = it - 1
                xs, bc = XS[1 - par], BC[1 - par]
                SG, EB, TR, YB = bank(4), bank(5), bank(6), bank(7)

                def filler(lo, hi):
                    if not panels:
                        return
                    for j in range(6):
                        a, b = max(lo, 48 * j), min(hi, 48 * j + 48)
                        if a < b:
                            P = P_SSM + j
                            if a == 48 * j:
                                begin(6 * it + P, 6 * it + (P + U_OF_P), 1)
                            mm = panel((P + U_OF_P) % 2, P % 2, UH, UL, a - 48 * j, b - 48 * j)
                            if b == 48 * j + 48:
                                mm.then_inc(pp_full, 1)

                for cnk in range(QB):
                    if scan:
                        l = slice(128 * cnk, 128 * cnk + 128)
                        if cnk == 0:
                            pe.wait_ge(sem("arow_in"), 64 * g + 64)
                            pe.wait_ge(sem("silu"), 6 * g + 5)
                            pe.wait_ge(sem("tables"), 3)
                            pe.wait_ge(sem("rms_ev"), g + 1)
                        pe.wait_ge(sem("hs"), 8 * g + (cnk + 1))
                        for h in range(HPG):
                            pe.matmul(SG[:, 128 * h:128 * h + 128], SEL[:, h], AROW[:, l], start=(h == 0), stop=False, skip_group_check=True)
                        mm = pe.matmul(SG, IDR[:], MASKS[:].rearrange("p h n -> p (h n)"), start=False, stop=True, skip_group_check=True)
                        mm.then_inc(sem("sg"), 1)
                        for h in range(HPG):
                            mm = pe.matmul(EB[:, 128 * h:128 * h + 128], SEL[:, 4 + h], AROW[:, l], start=True, stop=True)
                        mm.then_inc(sem("eb"), 1)
                        pe.wait_ge(sem("ms"), 8 * g + (cnk + 1))
                        pe.transpose(TR[:, 0:128], xs[:, 0, l], IDF[:])
                        pe.transpose(TR[:, 128:256], xs[:, 1, l], IDF[:])
                        pe.transpose(TR[:, 256:384], bc[:, 0, l], IDF[:])
                        pe.matmul(TR[:, 384:512], bc[:, 0, l], bc[:, 1, l], start=True, stop=True).then_inc(sem("tr"), 1)
                    filler(36 * cnk, 36 * cnk + 18)
                    if scan:
                        pe.wait_ge(sem("ms"), 8 * g + (cnk + 2))
                        pe.wait_ge(sem("yev"), 8 * g + (cnk + 1))
                        for h in range(HPG):
                            o, t = YB[:, 128 * h:128 * h + 128], slice(128 * (h // 2), 128 * (h // 2) + 128)
                            pe.matmul(o, XD[:, t], MS[:, h], start=True, stop=False)
                            mm = pe.matmul(o, HS[:, t], CS[:, h], start=False, stop=True)
                        mm.then_inc(sem("yps"), 1)
                        if cnk < QB - 1:
                            pe.matmul(SG[:, 0:256], BT[:], XE[:], start=True, stop=True).then_inc(sem("st"), 1)
                    filler(36 * cnk + 18, 36 * cnk + 36)
                if scan:
                    pe.wait_ge(sem("ysq"), g + 1)
                    pe.wait_ge(sem("hs"), 8 * g + 9)
                    for h in range(2):
                        mm = pe.matmul(bank(4 + h), ONESF[:], SQ2[:, h * HALF:(h + 1) * HALF], start=True, stop=True)
                    mm.then_inc(sem("rms"), 1)
                else:
                    pe.wait_ge(sem("dtrows"), 1)
                    for q, v in enumerate((DTT, ACS, DDE)):
                        for j in range(QB):
                            mm = pe.transpose(bank(4, 2)[:, 256 * q + 32 * j:256 * q + 32 * j + 32],
                                              v[96:128, 128 * j:128 * j + 128], IDF[96:128, 96:128])
                    mm.then_inc(sem("tab_ps"), 1)

            rounds(pe, ssm)
            for f, (xh, xl, s_) in enumerate(((UH, UL, "ulp"), (HH, HL, "hlp"))):
                with pe.Fori(0, KT // 2) as r:
                    for k in range(2):
                        P = P_OUT + 8 * f + k
                        begin(2 * r + P, 2 * r + (P + U_OF_P), 1)
                        w0 = KT if f == 0 else 0
                        panel((P + U_OF_P) % 2, P % 2, xh, xl,
                              wait_k=(lambda i: pe.wait_ge(sem(s_), w0 + i + 1)) if k == 0 else None).then_inc(pp_full, 1)
            stats(2)
            mlp(1, P_MLP1, 40)
            stats(3)
            for t in range(QB):
                if t % 4 == 0:
                    pe.wait_ge(sem("rfin"), KT * (t // 4 + 1))
                pe.wait_ge(pp_free, U_END + t + 1)
                for k in range(KT):
                    mm = pe.transpose(pp((U_END + t) % 2)[:, k * 128:(k + 1) * 128], R[:, k, t * 128:(t + 1) * 128], IDF[:])
                mm.then_inc(pp_full, 1)


        def uses(t):
            s, i = divmod(t, QB)
            return 12 * s + [0, 1, 2, 3, 4, 6, 8, 10][i]

        EVICT = {2: 0, 3: 1, 4: 2, 6: 3, 7: 4}

        @block.scalar
        def _(act):
            own = Count(sem("act_c"))

            def link(ins):
                own.inc(ins)
                act.wait_ge(own.sem, own.n)

            act.sem_inc(sem("exp"), 1)
            act.sem_inc(sem("pth"), 1)
            act.sem_inc(sem("pv_ev"), 1)
            act.sem_inc(sem("yout"), 32)
            act.wait_ge(sem("vecs"), 4)
            act.activation(COND[:, 8:16], COND[:, 8:16], ACT.Tanh).then_inc(sem("condt"), 1)
            act.wait_ge(sem("mod0"), 2)
            for k in range(KT):
                act.wait_ge(pp_full, k + 1)
                if k >= 2:
                    act.wait_ge(sem("ul"), k - 1)
                    act.wait_ge(xsp0[k % 2], 16 * (k // 2))
                ps = pp(k % 2)
                link(act.activation(XU[:, k % 2], ps, ACT.Identity, bias=MOD[:, k:k + 1], scale=COLS[:, 3, 0, k:k + 1]))
                act.activation(UH[:, k], XU[:, k % 2], ACT.Copy).then_inc(sem("uh"), 1)
                act.activation(RST[:, k % 2], ps, ACT.Copy, scale=ALPHA).then_inc(pp_free, 1)
                act.wait_ge(pp_free, k + 3)
                act.dma_start(XSCR[0, k], RST[:, k % 2]).then_inc(xsp0[k % 2], 16)

            q96 = slice(96, 128)

            def log1p_exp(n, m, e, u, l):
                act.wait_ge(sem("sp_m"), n + 1)
                act.activation(e[q96], m[q96], ACT.Exp, scale=-1.0).then_inc(sem("sp_e"), 1)
                act.wait_ge(sem("sp_u"), n + 1)
                link(act.activation(l[q96], u[q96], ACT.Ln))
                act.wait_ge(sem("sp_r"), n + 1)
                act.activation(u[q96], l[q96], ACT.Exp, scale=-1.0).then_inc(sem("sp_l"), 1)

            log1p_exp(0, FM, FE, FU, FL)
            act.wait_ge(sem("fcum"), 1)
            act.activation(FNH[q96], FC[q96], ACT.Copy).then_inc(sem("fnh"), 1)
            act.wait_ge(sem("fnh"), 1)
            act.dma_start(CSCR[:, 0, :], FNH[112:128, :].bitcast(F32)).then_inc(sem("cscr"), 16)
            act.wait_ge(sem("fnl"), 1)
            act.dma_start(CSCR[:, 1, :], FNL[112:128, :].bitcast(F32)).then_inc(sem("cscr"), 16)
            act.wait_ge(sem("cscr"), 32)
            act.wait_ge(sem("consts"), 2)

            def load_ncr(pair):
                for s in range(2):
                    src = CSCR[ds(2 * pair + s, 1)].rearrange("a b n -> (a b) n")
                    act.dma_start(NCR[64 * s:64 * s + 2, :].bitcast(F32), src).then_inc(sem("ncr_in"), 16)

            load_ncr(0)

            def fox(it, par, panels, attend):
                a = it - 1
                u0 = 4 * it + U_FOX

                def take(j):
                    act.wait_ge(pp_full, u0 + (j + 1))
                    if j == 2:
                        act.activation(VT[:], pp(0), ACT.Copy).then_inc(pp_free, 1)
                        act.wait_ge(pp_full, u0 + 4)
                        act.activation(VH[:, par].rearrange("p a b -> p (a b)"), pp(0), ACT.Copy).then_inc(sem("qkvh"), 1)
                    else:
                        act.activation((QH, KH)[j][:, par], pp(0), ACT.Copy, scale=(DH ** -0.5, 1.0)[j]).then_inc(sem("qkvh"), 1)

                def hi(t, b):
                    nb = min(4, t % QB + 1 - 4 * b)
                    act.wait_ge(sem("pt"), 24 * a + (uses(t) + b + 1))
                    act.activation(PTH[:, 4 * b:4 * b + nb], bank(4)[:, 0:128 * nb].rearrange("p (a b) -> p a b", b=128),
                                   ACT.Copy).then_inc(sem("pth"), 1)

                for t in range(18):
                    if attend:
                        if 1 <= t <= 16:
                            hi(t - 1, 0)
                        if t >= 2 and (t - 2) % 4 == 3:
                            s, i = divmod(t - 2, QB)
                            rows = slice(64 * s, 64 * s + 64)
                            act.wait_ge(sem("pv"), 16 * a + (t - 1))
                            dst = Y0[rows, ds(a, 1), 128 * (i - 3):128 * (i + 1)]
                            act.activation(dst, bank(6)[rows].unsqueeze(1), ACT.Copy).then_inc(sem("pv_ev"), 1)
                        if t < 16:
                            n = 128 * (t % QB + 1)
                            act.wait_ge(sem("mx"), 16 * a + (t + 1))
                            act.wait_ge(sem("p"), 16 * a + (t + 1))
                            act.activation(PE_[:, 0:n], bank(2, 2)[:, 0:n], ACT.Exp, bias=NEGM[:, t % 2:t % 2 + 1],
                                           accum_out=RSUM[:, t % 2:t % 2 + 1]).then_inc(sem("exp"), 1)
                            if t == 15 and panels:
                                load_ncr(it)
                        if 1 <= t <= 16 and (t - 1) % QB >= 4:
                            hi(t - 1, 1)
                    if panels and t in (5, 11, 17):
                        take(t // 6)

            rounds(act, fox)

            def reload(n):
                for m in range(KT):
                    act.dma_start(R[:, m], XSCR[n, m]).then_inc(sem(f"r_in{m}"), 16)

            def squares(n, U):
                for m in range(KT):
                    act.wait_ge(pp_free, U + m + 3)
                    if m == 0:
                        act.activation(TB[:], R[:, 0], ACT.Square).then_inc(sem("sqa"), 1)
                        continue
                    for h in range(2):
                        if 14 * n + 2 * (m - 1) + h > 0:
                            act.wait_ge(sem("sqd"), 14 * n + 2 * (m - 1) + h)
                        act.activation(SQ[:], R[:, m, h * HALF:(h + 1) * HALF], ACT.Square).then_inc(sem("sqa"), 1)

            def norm(n, to_scratch=None, last=False):
                for h in range(2):
                    v = slice(h * HALF, (h + 1) * HALF)
                    act.wait_ge(sem("lv"), 2 * n + h + 1)
                    link(act.activation(LV[:, v], LV[:, v], ACT.Ln))
                    act.activation(LA[:, v], LV[:, v], ACT.Exp, scale=-0.5).then_inc(sem("la"), 1)
                for h in range(2):
                    v = slice(h * HALF, (h + 1) * HALF)
                    for k in range(KT):
                        act.wait_ge(sem("xn"), 16 * n + 8 * h + k + 1)
                        if last:
                            act.activation(R[:, k, v], R[:, k, v], ACT.Identity, bias=VEC2[:, 56 + k:57 + k],
                                           scale=VEC2[:, 40 + k:41 + k]).then_inc(sem("rfin"), 1)
                            continue
                        e = 8 * h + k
                        act.wait_ge(sem("ul"), 8 + 16 * n + e - 1)
                        link(act.activation(U32[:, k % 2], R[:, k, v], ACT.Identity, bias=COLS[:, n, 1, k:k + 1],
                                            scale=COLS[:, n, 0, k:k + 1]))
                        act.activation(UH[:, k, v], U32[:, k % 2], ACT.Copy).then_inc(sem("uh"), 1)
                if last:
                    return
                for k in range(KT):
                    act.activation(R[:, k], R[:, k], ACT.Identity, bias=COLS[:, n, 3, k:k + 1],
                                   scale=COLS[:, n, 2, k:k + 1]).then_inc(sem("rp"), 1)
                    if to_scratch is not None:
                        act.wait_ge(sem("rp"), 8 * n + k + 1)
                        act.dma_start(XSCR[to_scratch, k], R[:, k]).then_inc(sem("xspill1"), 16)

            for q in xsp0:
                act.wait_ge(q, 8 * KT)
            reload(0)
            squares(0, U_WO)
            norm(0)

            def mlp_act(layer, U0):
                c0 = own.n
                with act.Fori(0, 4) as f:
                    with act.Fori(0, KT // 2) as r:
                        own.at(c0 + 8 * f + 2 * r)
                        for k in range(2):
                            U = 16 * f + 2 * r + (U0 + k)
                            T = (TA, TB)[k]
                            act.wait_ge(pp_full, U + 1)
                            act.wait_ge(pp_free, U + 2)
                            act.wait_ge(sem("hl"), 8 * f + 2 * r + (32 * layer + k + 1))
                            act.activation(T[:], pp((U0 + k) % 2), ACT.Relu).then_inc(pp_free, 1)
                            act.wait_ge(pp_free, U + 3)
                            link(act.activation(T[:], T[:], ACT.Square))
                            act.activation(HH[:, ds(2 * r + k, 1)], T[:].unsqueeze(1), ACT.Copy).then_inc(sem("hh"), 1)
                own.at(c0 + 32)

            mlp_act(0, P_MLP0 + U_OF_P)
            squares(1, P_DT - KT + U_OF_P)
            norm(1, to_scratch=1)

            act.activation(SMALL[q96, 3:4], SMALL[q96, 2:3], ACT.Exp).then_inc(sem("alog"), 1)
            log1p_exp(1, DDE, DE, DU, DL)
            act.wait_ge(sem("acs"), 1)
            act.activation(EAC[q96], ACS[q96], ACT.Exp).then_inc(sem("eac"), 1)
            act.activation(DDE[q96], DDE[q96], ACT.Exp).then_inc(sem("dde"), 1)
            act.wait_ge(sem("eac"), 1)
            for n, src in enumerate((ACS, EAC)):
                act.activation(RWH[n][q96], src[q96], ACT.Copy).then_inc(sem("rwh"), 1)
            act.wait_ge(sem("rwl"), 2)
            act.wait_ge(sem("rwh"), 2)
            for n, t in enumerate((RWH[0], RWL[0], RWH[1], RWL[1])):
                act.dma_start(ASCR[n], t[q96].bitcast(F32)).then_inc(sem("ascr"), 16)

            def load_arow(g):
                for q in range(4):
                    act.dma_start(AROW[4 * q:4 * q + 4, :].bitcast(F32), ASCR[q, ds(4 * g, 4), :]).then_inc(sem("arow_in"), 16)

            def ssm(it, par, panels, scan):
                g = it - 1
                gp = 1 - par

                def take(j):
                    U = 6 * it + (P_SSM + j + U_OF_P)
                    ps = pp((P_SSM + j + U_OF_P) % 2)
                    act.wait_ge(pp_full, U + 1)
                    act.wait_ge(sem("silu"), 6 * it + (j + 1))
                    if j < 4:
                        col = (it + 16, it + 24, 2 * it, 2 * it + 1)[j]
                        act.activation(XP[:, 3:3 + S], ps, ACT.Copy).then_inc(pp_free, 1)
                        act.wait_ge(pp_free, U + 3)
                        act.activation(CT[:], XP[:, 3:3 + S], ACT.Identity, bias=CBH[:, ds(col, 1)],
                                       scale=VEC3[:, ds(col + 96, 1)]).then_inc(sem("ct"), 1)
                        act.wait_ge(sem("conv"), 4 * it + (j + 1))
                        act.activation(TT[:], CT[:], ACT.Tanh).then_inc(sem("tt"), 1)
                    else:
                        act.activation(CT[:], ps, ACT.Copy, scale=0.5).then_inc(sem("zh"), 1)
                        act.activation(TT[:], ps, ACT.Tanh, scale=0.5).then_inc(pp_free, 1)

                for cnk in range(QB):
                    if scan:
                        act.wait_ge(sem("tr"), 8 * g + (cnk + 1))
                        act.activation(BT[:], bank(6)[:, 256:384], ACT.Copy).then_inc(sem("bt"), 1)
                        act.wait_ge(sem("seg"), 8 * g + (cnk + 1))
                        act.activation(ES[:], ES[:], ACT.Exp).then_inc(sem("es"), 1)
                    if panels and cnk in EVICT:
                        take(EVICT[cnk])
                    if not panels and cnk == 3:
                        act.wait_ge(sem("yout"), 32 * GROUPS)
                        act.wait_ge(sem("silu"), 6 * GROUPS + 1)
                        act.wait_ge(sem("yev"), 8 * (GROUPS - 1) + 1)
                        for m in range(KT):
                            act.dma_start(Y0[:, m], YSCR[m]).then_inc(sem(f"y0_in{m}"), 16)
                if scan and panels:
                    act.wait_ge(sem("yps"), 8 * g + 8)
                    load_arow(it)
                if panels:
                    take(5)
                if not scan:
                    act.wait_ge(sem("ascr"), 64)
                    act.wait_ge(sem("ssm_consts"), 1)
                    load_arow(0)
                if scan:
                    act.wait_ge(sem("yev"), 8 * g + 9)
                    act.activation(SQ2[:], YR[:, gp, 0], ACT.Square).then_inc(sem("ysa"), 1)
                    act.activation(RS2[:], YR[:, gp, 1], ACT.Square).then_inc(sem("ysa"), 1)
                    act.wait_ge(sem("rms_ev"), g + 2)
                    act.activation(RS2[:], RS2[:], ACT.Ln).then_inc(sem("rln"), 1)
                    act.wait_ge(sem("rln"), g + 1)
                    act.activation(RS2[:], RS2[:], ACT.Exp, scale=-0.5).then_inc(sem("rsa"), 1)
                    for t in range(2):
                        act.wait_ge(sem("yfin"), 2 * g + (t + 1))
                        act.dma_start(YSCR[ds(2 * g + t, 1)].rearrange("a p n -> p a n"), YR[:, gp, t:t + 1]).then_inc(sem("yout"), 16)

            rounds(act, ssm)
            act.wait_ge(sem("yout"), 32 + 256)
            for m in range(KT):
                act.dma_start(Y1[:, m], YSCR[KT + m]).then_inc(sem(f"y1_in{m}"), 16)
            reload(1)
            squares(2, P_MLP1 - KT + U_OF_P)
            norm(2)
            mlp_act(1, P_MLP1 + U_OF_P)
            squares(3, P_END - KT + U_OF_P)
            norm(3, last=True)
            outd = [sem("out_even"), sem("out_odd")]
            for t in range(QB):
                act.wait_ge(pp_full, U_END + t + 1)
                if t >= 2:
                    act.wait_ge(outd[t % 2], 16 * (t // 2))
                act.activation(OST[:, t % 2], pp((U_END + t) % 2), ACT.Copy).then_inc(pp_free, 1)
                act.wait_ge(pp_free, U_END + t + 3)
                act.dma_start(out[0, 128 * t:128 * t + 128, :], OST[:, t % 2]).then_inc(outd[t % 2], 16)
            for q in outd:
                act.wait_ge(q, 8 * QB)

        @block.vector
        def _(dve):
            own = Count(sem("dve_c"))

            def link(ins):
                own.inc(ins)
                dve.wait_ge(own.sem, own.n)

            dve.sem_inc(pp_free, 2)
            dve.sem_inc(ada_ev, 2)
            dve.sem_inc(sem("ptl"), 1)
            dve.sem_inc(sem("p"), 1)
            dve.sem_inc(sem("hl"), 2)
            for s in ("hs", "ms", "yev", "rms_ev", "silu"):
                dve.sem_inc(sem(s), 1)
            dve.memset(SMALL[:], 0.0).then_inc(sem("small_z"), 1)
            dve.wait_ge(sem("vec_ps"), 1)
            for n, v in enumerate((VEC1, VEC2, VEC3)):
                link(dve.tensor_copy(v[:], bank(4)[:, 128 * n:128 * n + v.shape[1]]))
            vecs = sem("vecs")
            dve.tensor_scalar(COND[:, 8:16], VEC1[:, 96:104], 0.5, None, ALU.mult).then_inc(vecs, 1)
            dve.tensor_scalar(VEC3[:], VEC3[:], 0.5, None, ALU.mult).then_inc(vecs, 1)
            dve.tensor_scalar(CBH[:], VEC2[:, 64:96], 0.5, None, ALU.mult).then_inc(vecs, 1)
            dve.tensor_scalar(COND[:, 0:8], VEC1[:, 96:104], 0.5, None, ALU.mult).then_inc(vecs, 1)
            dve.wait_ge(vecs, 4)
            dve.wait_ge(sem("condt"), 1)
            dve.scalar_tensor_tensor(out=COND[:, 0:8], in0=COND[:, 8:16], scalar=1.0, in1=COND[:, 0:8],
                                     op0=ALU.add, op1=ALU.mult).then_inc(sem("cond"), 1)
            dve.wait_ge(sem("small_in"), 64)
            for s in range(2):
                rows = slice(64 * s, 64 * s + 64)
                dve.tensor_copy(DCOL[rows], DALL[rows].rearrange("p (t s) -> p t s", s=2)[:, :, s]).then_inc(sem("dcol"), 1)
            dve.wait_ge(sem("ada0_ps"), 1)
            dve.tensor_tensor(MOD[:, 0:16], bank(5)[:, 0:16], VEC1[:, 0:16], ALU.add).then_inc(sem("mod0"), 1)
            dve.wait_ge(sem("mod0"), 1)
            dve.tensor_scalar(COLS[:, 3, 0], MOD[:, 8:16], 1.0, None, ALU.add).then_inc(sem("mod0"), 1)
            for k in range(KT):
                dve.wait_ge(sem("uh"), k + 1)
                dve.tensor_tensor(UL[:, k], XU[:, k % 2], UH[:, k].bitcast(F32), ALU.subtract).then_inc(sem("ul"), 1)

            q96 = slice(96, 128)

            def log1p_exp(n, z, m, e, u, l):
                dve.scalar_tensor_tensor(out=m[q96], in0=z[q96], scalar=-1.0, in1=z[q96], op0=ALU.mult, op1=ALU.max).then_inc(sem("sp_m"), 1)
                dve.wait_ge(sem("sp_e"), n + 1)
                dve.tensor_scalar(u[q96], e[q96], 1.0, None, ALU.add).then_inc(sem("sp_u"), 1)
                dve.wait_ge(sem("sp_u"), n + 1)
                dve.scalar_tensor_tensor(out=m[q96], in0=u[q96], scalar=-1.0, in1=e[q96], op0=ALU.add, op1=ALU.subtract).then_inc(sem("sp_r"), 1)
                dve.wait_ge(sem("sp_l"), n + 1)
                dve.wait_ge(sem("sp_r"), n + 1)
                link(dve.tensor_tensor(m[q96], m[q96], u[q96], ALU.mult))
                link(dve.tensor_tensor(l[q96], l[q96], m[q96], ALU.subtract))

            dve.wait_ge(pp_full, U_F + 1)
            for q in xsp0:
                dve.wait_ge(q, 8 * KT)
            dve.tensor_scalar(FZ[q96], pp(0)[q96], SMALL[q96, 0:1], None, ALU.add).then_inc(pp_free, 1)
            dve.wait_ge(pp_free, U_F + 3)
            log1p_exp(0, FZ, FM, FE, FU, FL)
            link(dve.tensor_scalar(FZ[q96], FZ[q96], -1.0, 0.0, ALU.mult, ALU.max))
            link(dve.tensor_tensor(FZ[q96], FZ[q96], FL[q96], ALU.add))
            link(dve.memset(FM[q96], 1.0))
            dve.tensor_tensor_scan(FC[q96], FM[q96], FZ[q96], 0.0, ALU.mult, ALU.add).then_inc(sem("fcum"), 1)
            dve.wait_ge(sem("fnh"), 1)
            dve.tensor_tensor(FNL[q96], FC[q96], FNH[q96].bitcast(F32), ALU.subtract).then_inc(sem("fnl"), 1)

            def ada(n):
                dve.wait_ge(ada_ps, n + 1)
                dve.tensor_tensor(MOD[:, ds(n + 16, 1)], bank(7)[:, 0:1], VEC1[:, ds(n + 16, 1)], ALU.add).then_inc(ada_ev, 1)

            def fox(it, par, panels, attend):
                a = it - 1
                u0 = 4 * it + U_FOX

                def take(j):
                    dve.wait_ge(sem("qkvh"), 3 * it + (j + 1))
                    if j == 0:
                        dve.scalar_tensor_tensor(out=QL[:, par], in0=pp(0), scalar=DH ** -0.5, in1=QH[:, par].bitcast(F32),
                                                 op0=ALU.mult, op1=ALU.subtract).then_inc(pp_free, 1)
                    elif j == 1:
                        dve.tensor_tensor(KL[:, par], pp(0), KH[:, par].bitcast(F32), ALU.subtract).then_inc(pp_free, 1)
                    else:
                        dve.tensor_tensor(VL[:, par].rearrange("p a b -> p (a b)"), pp(0),
                                          VH[:, par].rearrange("p a b -> p (a b)").bitcast(F32), ALU.subtract).then_inc(pp_free, 1)
                    ada(3 * it + j)

                def lo(t, b):
                    nb = min(4, t % QB + 1 - 4 * b)
                    dve.wait_ge(sem("pt"), 24 * a + (uses(t) + b + 1))
                    dve.tensor_copy(PTL[:, 4 * b:4 * b + nb], bank(5)[:, 0:128 * nb].rearrange("p (a b) -> p a b", b=128)).then_inc(sem("ptl"), 1)

                for t in range(18):
                    if attend:
                        n = 128 * (t % QB + 1)
                        v = slice(t % 2, t % 2 + 1)
                        if t < 16:
                            dve.wait_ge(sem("sc"), 16 * a + (t + 1))
                            dve.tensor_reduce(NEGM[:, v], bank(2, 2)[:, 0:n], AX.X, ALU.max, negate=True).then_inc(sem("mx"), 1)
                        if 1 <= t <= 16:
                            lo(t - 1, 0)
                            if (t - 1) % QB >= 4:
                                lo(t - 1, 1)
                        if t < 16:
                            dve.wait_ge(sem("exp"), 16 * a + (t + 2))
                            dve.reciprocal(RINV[:, v], RSUM[:, v]).then_inc(sem("rinv"), 1)
                            dve.wait_ge(sem("rinv"), 16 * a + (t + 1))
                            dve.tensor_scalar(PH[:, 0:n], PE_[:, 0:n], RINV[:, v], None, ALU.mult).then_inc(sem("ph"), 1)
                            dve.wait_ge(sem("ph"), 16 * a + (t + 1))
                            dve.scalar_tensor_tensor(out=PL[:, 0:n], in0=PE_[:, 0:n], scalar=RINV[:, v], in1=PH[:, 0:n].bitcast(F32),
                                                     op0=ALU.mult, op1=ALU.subtract).then_inc(sem("p"), 1)
                    if panels and t in (5, 11, 17):
                        take(t // 6)

            rounds(dve, fox)

            def columns(n, g_at, b_at, sc_at, sh_at):
                C = COLS[:, n]
                g, b = VEC2[:, g_at:g_at + 8], VEC2[:, b_at:b_at + 8]
                link(dve.tensor_scalar(C[:, 3], MOD[:, sc_at:sc_at + 8], 1.0, None, ALU.add))
                link(dve.tensor_tensor(C[:, 0], C[:, 3], g, ALU.mult))
                link(dve.tensor_tensor(C[:, 1], C[:, 3], b, ALU.mult))
                link(dve.tensor_tensor(C[:, 1], C[:, 1], MOD[:, sh_at:sh_at + 8], ALU.add))
                link(dve.tensor_scalar(C[:, 2], g, ALPHA, None, ALU.mult))
                link(dve.tensor_scalar(C[:, 3], b, ALPHA, None, ALU.mult))

            def gate(n, at_):
                link(dve.tensor_scalar(G1[:, n], MOD[:, at_:at_ + 8], 1.0, None, ALU.add))

            def add_up(n, m, U, ada_n=None):
                dve.wait_ge(pp_full, U + 1)
                if n % 2 == 0:
                    dve.wait_ge(sem(f"r_in{m}"), 16 * (n // 2 + 1))
                dve.scalar_tensor_tensor(out=R[:, m], in0=pp(U % 2), scalar=G1[:, n, m:m + 1], in1=R[:, m],
                                         op0=ALU.mult, op1=ALU.add).then_inc(pp_free, 1)
                if ada_n is not None:
                    ada(ada_n)
                dve.wait_ge(pp_free, U + 3)
                if m == 1:
                    link(dve.tensor_tensor(TA[:], R[:, 0], R[:, 1], ALU.add))
                elif m > 1:
                    link(dve.tensor_tensor(TA[:], TA[:], R[:, m], ALU.add))
                if m > 0:
                    for h in range(2):
                        v = slice(h * HALF, (h + 1) * HALF)
                        dve.wait_ge(sem("sqa"), 15 * n + 2 * m + h)
                        dve.tensor_tensor(TB[:, v], TB[:, v], SQ[:], ALU.add).then_inc(sem("sqd"), 1)
                        dve.wait_ge(sem("sqd"), 14 * n + 2 * (m - 1) + h + 1)

            def norm(n, last=False):
                dve.wait_ge(sem("stats"), n + 1)
                for h in range(2):
                    v = slice(h * HALF, (h + 1) * HALF)
                    link(dve.tensor_scalar(LM[:, v], bank(4 + h), 1.0 / D, None, ALU.mult))
                    link(dve.tensor_tensor(LS[:, v], LM[:, v], LM[:, v], ALU.mult))
                    link(dve.scalar_tensor_tensor(out=LV[:, v], in0=bank(6 + h), scalar=1.0 / D, in1=LS[:, v], op0=ALU.mult, op1=ALU.subtract))
                    dve.tensor_scalar(LV[:, v], LV[:, v], 0.0, EPS, ALU.max, ALU.add).then_inc(sem("lv"), 1)
                for h in range(2):
                    v = slice(h * HALF, (h + 1) * HALF)
                    dve.wait_ge(sem("la"), 2 * n + h + 1)
                    link(dve.scalar_tensor_tensor(out=LB[:, v], in0=LM[:, v], scalar=-1.0, in1=LA[:, v], op0=ALU.mult, op1=ALU.mult))

                    def low(k):
                        dve.wait_ge(sem("uh"), 8 + 16 * n + 8 * h + k + 1)
                        dve.tensor_tensor(UL[:, k, v], U32[:, k % 2], UH[:, k, v].bitcast(F32), ALU.subtract).then_inc(sem("ul"), 1)

                    for k in range(KT):
                        link(dve.tensor_tensor(R[:, k, v], R[:, k, v], LA[:, v], ALU.mult))
                        dve.tensor_tensor(R[:, k, v], R[:, k, v], LB[:, v], ALU.add).then_inc(sem("xn"), 1)
                        if k >= 1 and not last:
                            low(k - 1)
                    if not last:
                        low(KT - 1)

            dve.wait_ge(ada_ev, 24 + 2)
            columns(0, 0, 16, 32, 24)
            gate(0, 16)
            for m in range(KT):
                add_up(0, m, U_WO + m, 24 + m)
            dve.wait_ge(ada_ev, 32 + 2)
            gate(1, 40)
            norm(0)

            def mlp_dve(layer, U0, n):
                def first(f, ada_too):
                    with dve.Fori(0, KT // 2) as r:
                        for k in range(2):
                            dve.wait_ge(sem("hh"), 8 * f + 2 * r + (32 * layer + k + 1))
                            dve.tensor_tensor(HL[:, ds(2 * r + k, 1)], (TA, TB)[k][:].unsqueeze(1),
                                              HH[:, ds(2 * r + k, 1)].bitcast(F32), ALU.subtract).then_inc(sem("hl"), 1)
                            if ada_too:
                                ada(16 * f + 2 * r + (32 + k))

                dve.wait_ge(sem("rp"), 8 * n)
                with dve.Fori(0, 3) as f:
                    first(f, layer == 0)
                    with dve.Fori(0, KT // 2) as r:
                        for k in range(2):
                            U = 16 * f + 2 * r + (U0 + 8 + k)
                            dve.wait_ge(pp_full, U + 1)
                            dve.wait_ge(pp_free, U + 2)
                            dve.scalar_tensor_tensor(out=R[:, ds(2 * r + k, 1)], in0=pp((U0 + k) % 2).unsqueeze(1),
                                                     scalar=G1[:, n, ds(2 * r + k, 1)], in1=R[:, ds(2 * r + k, 1)],
                                                     op0=ALU.mult, op1=ALU.add).then_inc(pp_free, 1)
                            if layer == 0:
                                ada(16 * f + 2 * r + (40 + k))
                first(3, False)
                if layer == 0:
                    dve.wait_ge(ada_ev, ADA_JOBS + 2)
                    columns(1, 32, 48, 56, 48)
                    columns(2, 8, 24, 80, 72)
                    gate(2, 64)
                    gate(3, 88)
                dve.wait_ge(pp_free, U0 + 56 + 2)
                for m in range(KT):
                    add_up(n, m, U0 + 56 + m)

            mlp_dve(0, P_MLP0 + U_OF_P, 1)
            norm(1)

            dve.memset(XP[:, 0:3], 0.0).then_inc(sem("xp0"), 1)
            dve.wait_ge(pp_full, P_DT + U_OF_P + 1)
            dve.tensor_scalar(DZ[q96], pp((P_DT + U_OF_P) % 2)[q96], SMALL[q96, 1:2], None, ALU.add).then_inc(pp_free, 1)
            dve.wait_ge(pp_free, P_DT + U_OF_P + 3)
            dve.wait_ge(sem("xspill1"), 16 * KT)
            dve.wait_ge(sem("ssm_consts"), 1)
            log1p_exp(1, DZ, DDE, DE, DU, DL)
            link(dve.scalar_tensor_tensor(out=DTT[q96], in0=DZ[q96], scalar=0.0, in1=DL[q96], op0=ALU.max, op1=ALU.add))
            dve.wait_ge(sem("alog"), 1)
            link(dve.tensor_scalar(SMALL[q96, 4:5], SMALL[q96, 3:4], -1.0, None, ALU.mult))
            link(dve.tensor_scalar(DZ[q96], DTT[q96], SMALL[q96, 4:5], None, ALU.mult))
            for j in range(QB):
                l = slice(128 * j, 128 * j + 128)
                scan_ = dve.tensor_tensor_scan(ACS[q96, l], ONESF[q96], DZ[q96, l], 0.0, ALU.mult, ALU.add)
            link(scan_)
            acs_c = ACS[q96].rearrange("p (c l) -> p c l", l=128)
            dve.tensor_tensor(DDE[q96].rearrange("p (c l) -> p c l", l=128), acs_c[:, :, 127:128].broadcast_to([32, QB, 128]),
                              acs_c, ALU.subtract).then_inc(sem("acs"), 1)
            for n, src in enumerate((ACS, EAC)):
                dve.wait_ge(sem("rwh"), n + 1)
                dve.tensor_tensor(RWL[n][q96], src[q96], RWH[n][q96].bitcast(F32), ALU.subtract).then_inc(sem("rwl"), 1)
            dve.wait_ge(sem("dde"), 1)
            dve.tensor_tensor(DDE[q96], DDE[q96], DTT[q96], ALU.mult).then_inc(sem("dtrows"), 1)
            link(dve.memset(HS[:], 0.0))

            def ssm(it, par, panels, scan):
                g = it - 1
                gp = 1 - par
                xs, bc = XS[gp], BC[gp]
                SG, EB, TR, YB = bank(4), bank(5), bank(6), bank(7)

                def heads(v, n=128):
                    return v.rearrange("p (h n) -> p h n", n=n)

                def per_head(tab, cnk, n):
                    return tab[:, cnk, ds(4 * g, HPG)].unsqueeze(2).broadcast_to([128, HPG, n])

                def take(j):
                    if j < 4:
                        col = (it + 16, it + 24, 2 * it, 2 * it + 1)[j]
                        dve.wait_ge(sem("ct"), 4 * it + (j + 1))
                        for tap in (2, 1, 0):
                            ins = dve.scalar_tensor_tensor(out=CT[:], in0=XP[:, tap:tap + S], scalar=VEC3[:, ds(col + 32 * tap, 1)],
                                                           in1=CT[:], op0=ALU.mult, op1=ALU.add)
                            if tap:
                                ins.then_inc(sem("tap"), 1)
                                dve.wait_ge(sem("tap"), 8 * it + (2 * j + 3 - tap))
                        ins.then_inc(sem("conv"), 1)
                        dve.wait_ge(sem("tt"), 4 * it + (j + 1))
                        dst = BC[par][:, j] if j < 2 else XS[par][:, j - 2]
                    else:
                        if not (isinstance(it, int) and it == 0):
                            dve.wait_ge(sem("yout"), 32 * it)
                        dve.wait_ge(pp_free, 6 * it + (P_SSM + j + U_OF_P + 3))
                        dst = YR[:, par, j - 4]
                    dve.scalar_tensor_tensor(out=dst, in0=TT[:], scalar=1.0, in1=CT[:], op0=ALU.add, op1=ALU.mult).then_inc(sem("silu"), 1)

                for cnk in range(QB):
                    if scan:
                        l = slice(128 * cnk, 128 * cnk + 128)
                        e = 8 * g + cnk
                        if cnk == 0:
                            dve.wait_ge(sem("tables"), 3)
                            dve.wait_ge(sem("silu"), 6 * g + 7)
                        dve.wait_ge(sem("sg"), e + 1)
                        dve.tensor_tensor(ES[:], heads(SG), per_head(TAC, cnk, 128), ALU.subtract).then_inc(sem("seg"), 1)
                        dve.wait_ge(sem("bt"), e + 1)
                        dve.tensor_tensor(heads(XD[:], 64), heads(TR[:, 0:256], 64), per_head(TDT, cnk, 64), ALU.mult)
                        dve.tensor_tensor(heads(XE[:], 64), heads(TR[:, 0:256], 64), per_head(TDE, cnk, 64), ALU.mult)
                        dve.wait_ge(sem("eb"), e + 1)
                        dve.tensor_tensor(CS[:], heads(EB), bc[:, 1, l].unsqueeze(1).broadcast_to([128, HPG, 128]), ALU.mult)
                        dve.wait_ge(sem("es"), e + 1)
                        dve.tensor_tensor(MS[:], ES[:], TR[:, 384:512].unsqueeze(1).broadcast_to([128, HPG, 128]), ALU.mult).then_inc(sem("ms"), 1)
                        dve.wait_ge(sem("yps"), e + 1)
                        for h in range(HPG):
                            t, rows = h // 2, slice(64 * (h % 2), 64 * (h % 2) + 64)
                            ins = dve.scalar_tensor_tensor(out=XD[rows, 128 * t:128 * t + 128], in0=xs[rows, t, l],
                                                           scalar=DCOL[rows, ds(2 * g + t, 1)], in1=YB[rows, 128 * h:128 * h + 128],
                                                           op0=ALU.mult, op1=ALU.add)
                        ins.then_inc(sem("yd"), 1)
                        dve.wait_ge(sem("yd"), e + 1)
                        dve.tensor_tensor(YR[:, gp, :, l], YR[:, gp, :, l], heads(XD[:]), ALU.mult).then_inc(sem("yev"), 1)
                        if cnk < QB - 1:
                            dve.tensor_tensor(heads(HT[:], 64), heads(HS[:], 64), heads(EB)[:, :, 127:128].broadcast_to([128, HPG, 64]),
                                              ALU.mult).then_inc(sem("ht"), 1)
                            dve.wait_ge(sem("ht"), 7 * g + (cnk + 1))
                            dve.wait_ge(sem("st"), 7 * g + (cnk + 1))
                            dve.tensor_tensor(HS[:], HT[:], SG[:, 0:256], ALU.add).then_inc(sem("hs"), 1)
                        else:
                            dve.memset(HS[:], 0.0).then_inc(sem("hs"), 1)
                        dve.wait_ge(sem("hs"), e + 2)
                    if panels and cnk in EVICT:
                        take(EVICT[cnk])
                if panels:
                    take(5)
                if not scan:
                    dve.wait_ge(sem("tab_ps"), 1)
                    for q, tab in enumerate((TDT, TAC, TDE)):
                        dve.tensor_copy(tab[:], bank(4, 2)[:, 256 * q:256 * q + 256].rearrange("p (c h) -> p c h", h=32)).then_inc(sem("tables"), 1)
                if scan:
                    dve.wait_ge(sem("ysa"), 2 * g + 2)
                    dve.tensor_tensor(SQ2[:], SQ2[:], RS2[:], ALU.add).then_inc(sem("ysq"), 1)
                    dve.wait_ge(sem("rms"), g + 1)
                    dve.tensor_scalar(RS2[:], bank(4, 2), 1.0 / 256, EPS, ALU.mult, ALU.add).then_inc(sem("rms_ev"), 1)
                    dve.wait_ge(sem("rsa"), g + 1)
                    for t in range(2):
                        dve.scalar_tensor_tensor(out=YR[:, gp, t], in0=YR[:, gp, t], scalar=VEC2[:, ds(2 * g + (96 + t), 1)],
                                                 in1=RS2[:], op0=ALU.mult, op1=ALU.mult).then_inc(sem("yfin"), 1)

            rounds(dve, ssm)
            for m in range(KT):
                U = P_OUT + m + U_OF_P
                dve.wait_ge(pp_full, U + 1)
                dve.wait_ge(sem(f"r_in{m}"), 32)
                dve.scalar_tensor_tensor(out=R[:, m], in0=pp(U % 2), scalar=G1[:, 2, m:m + 1], in1=R[:, m],
                                         op0=ALU.mult, op1=ALU.add).then_inc(pp_free, 1)
            dve.wait_ge(pp_free, P_OUT + KT + U_OF_P + 2)
            for m in range(KT):
                add_up(2, m, P_OUT + KT + m + U_OF_P)
            norm(2)
            mlp_dve(1, P_MLP1 + U_OF_P, 3)
            norm(3, last=True)


_INPUTS = ["x", "c", "ada_w", "ada_b", "ln_mix_g", "ln_mix_b", "ln_mlp_g", "ln_mlp_b", "mlp_w1", "mlp_w2",
           "fox_w_in", "fox_b_f", "fox_w_o", "ssm_w_in", "ssm_conv_w", "ssm_conv_b", "ssm_dt_bias",
           "ssm_a_log", "ssm_d", "ssm_norm_w", "ssm_w_out"]


def kernel(**inputs):
    import numpy as _np
    import concourse.bacc as _bacc
    from concourse import mybir as _mybir
    from concourse.bass_utils import run_bass_kernel_spmd as _run

    nc = _bacc.Bacc("TRN2", target_bir_lowering=False, num_devices=1)
    arrays, args = {}, []
    for name in _INPUTS:
        a = _np.ascontiguousarray(inputs[name])
        arrays[f"in_{name}_dram"] = a
        args.append(nc.dram_tensor(f"in_{name}_dram", a.shape, _mybir.dt.from_np(a.dtype), kind="ExternalInput").ap())
    args.append(nc.dram_tensor("out_0_dram", (1, S, D), _mybir.dt.float32, kind="ExternalOutput").ap())
    build(nc, *args)
    r = _run(nc, [arrays], core_ids=[0])
    return r.results[0]["out_0_dram"]
```

```python
import numpy as np

import concourse.bass as bass
from concourse import mybir

F32 = mybir.dt.float32
F32R = mybir.dt.float32r
ALU = mybir.AluOpType
ACT = mybir.ActivationFunctionType
AX = mybir.AxisListType
ds = bass.ds

P128 = 128
D = 1024
S = 1024
KT = D // P128
HALF = 512
FF = 4 * D
HEADS, DH = 16, 64
PAIRS = HEADS // 2
QB = S // P128
DI = 2 * D
GROUPS = 8
NSTATE = 128
HPG = 4
DT0 = DI + DI + 2 * GROUPS * NSTATE
MASKED = -(2.0 ** 100)
EPS = 1e-5
ALPHA = (2.0 * 2) ** 0.25

P_FOX = 1
P_WO = P_FOX + 3 * PAIRS
P_MLP0 = P_WO + KT
P_DT = P_MLP0 + 64
P_SSM = P_DT + 1
P_OUT = P_SSM + 6 * GROUPS
P_MLP1 = P_OUT + 2 * KT
P_END = P_MLP1 + 64
U_F = 8
U_FOX = U_F + 1
U_WO = U_FOX + 4 * PAIRS
U_OF_P = U_WO - P_WO
U_END = P_END + U_OF_P
ADA_JOBS = 80


class Count:

    def __init__(self, sem):
        self.sem, self.base, self.k = sem, 0, 0

    @property
    def n(self):
        return self.base + self.k

    def at(self, base):
        self.base, self.k = base, 0

    def inc(self, ins):
        ins.then_inc(self.sem, 1)
        self.k += 1


def rounds(eng, work):
    work(0, 0, True, False)
    work(1, 1, True, True)
    with eng.Fori(0, 3) as r:
        work(2 * r + 2, 0, True, True)
        work(2 * r + 3, 1, True, True)
    work(8, 0, False, True)


def build(nc, x, c, ada_w, ada_b, ln_mix_g, ln_mix_b, ln_mlp_g, ln_mlp_b, mlp_w1, mlp_w2,
          fox_w_in, fox_b_f, fox_w_o, ssm_w_in, ssm_conv_w, ssm_conv_b, ssm_dt_bias,
          ssm_a_log, ssm_d, ssm_norm_w, ssm_w_out, out):
    base = (nc.sbuf_base + 31) // 32 * 32
    top = [base]

    def place(name, shape, dt, off):
        return nc.alloc_sbuf_tensor_at(name, shape, dt, offset=off)

    def keep(name, shape, dt=F32):
        off = top[0]
        top[0] += (int(np.prod(shape[1:])) * 4 + 31) // 32 * 32
        return place(name, shape, dt, off)

    UH, UL = keep("UH", [128, KT, S], F32R), keep("UL", [128, KT, S], F32R)
    RAW = keep("RAW", [128, 2, KT, 128])
    WH, WL = keep("WH", [128, 2, KT, 128], F32R), keep("WL", [128, 2, KT, 128], F32R)
    ADARAW, ADAACC = keep("ADARAW", [128, KT, 128]), keep("ADAACC", [128, 2, 128])
    IDF, IDR = keep("IDF", [128, 128]), keep("IDR", [128, 128], F32R)
    ONESF = keep("ONESF", [128, 128])
    MASKA = keep("MASKA", [128, 128], F32R)
    ONES2 = keep("ONES2", [128, 128], F32R)
    VEC1, VEC2, VEC3 = keep("VEC1", [128, 104]), keep("VEC2", [128, 112]), keep("VEC3", [128, 128])
    MOD = keep("MOD", [128, 96])
    COND = keep("COND", [128, 16])
    COLS = keep("COLS", [128, 4, 4, 8])
    G1 = keep("G1", [128, 4, 8])
    CBH = keep("CBH", [128, 32])
    DCOL = keep("DCOL", [128, 16])
    DALL = keep("DALL", [128, 32])
    SMALL = keep("SMALL", [128, 16])
    NEGM, RSUM, RINV = keep("NEGM", [128, 8]), keep("RSUM", [128, 8]), keep("RINV", [128, 8])
    OSUM = keep("OSUM", [64, 256])
    W0 = top[0]
    K = 1024

    def at(name, shape, kb, dt=F32):
        return place(name, shape, dt, W0 + int(kb * K))

    HH, HL = at("HH", [128, KT, S], 0, F32R), at("HL", [128, KT, S], 32, F32R)
    Y0, Y1 = at("Y0", [128, KT, S], 0), at("Y1", [128, KT, S], 32)
    R = at("R", [128, KT, S], 64)
    TA, TB, SQ = at("TA", [128, S], 96), at("TB", [128, S], 100), at("SQ", [128, S], 104)
    LA, LB, LM = at("LA", [128, S], 0), at("LB", [128, S], 4), at("LM", [128, S], 12)
    U32 = at("U32", [128, 2, HALF], 8)
    LV, LS = at("LV", [128, S], 16), at("LS", [128, S], 20)
    XIN = at("XIN", [128, KT, D], 0)
    ADA0 = at("ADA0", [128, KT, 2 * D], 32)
    RST = at("RST", [128, 2, S], 96)
    XU = at("XU", [128, 2, S], 32)
    VIN = at("VIN", [128, 3, 128], 104)
    QH, QL = at("QH", [128, 2, S], 32, F32R), at("QL", [128, 2, S], 40, F32R)
    KH, KL = at("KH", [128, 2, S], 48, F32R), at("KL", [128, 2, S], 56, F32R)
    VV = at("VV", [128, 2, QB, 2, 2, DH], 64, F32R)
    VT = at("VT", [128, S], 80)
    PE_ = at("PEXP", [128, S], 84)
    PN = at("PN", [128, 2, S], 88)
    PT = at("PT", [128, QB, 2, 128], 96, F32R)
    NCR = at("NCR", [128, S], 104, F32R)
    FZ, FM, FE, FU = (at(n, [128, S], 84 + 4 * i) for i, n in enumerate(("FZ", "FM", "FE", "FU")))
    FL, FC = at("FL", [128, S], 100), at("FC", [128, S], 92)
    FNH, FNL = at("FNH", [128, S], 36, F32R), at("FNL", [128, S], 44, F32R)
    OST = at("OST", [128, 2, D], 24)
    XS = [at("XS0", [128, 2, S], 0), at("XS1", [128, 2, S], 48)]
    BC = [at("BC0", [128, 2, S], 8), at("BC1", [128, 2, S], 56)]
    XP = at("XP", [128, 3 + S + 1], 16)
    CT, TT = at("CT", [128, S], 20.25), at("TT", [128, S], 24.25)
    YR = at("YR", [128, 2, 2, S], 32)
    ES, MS, CS = at("ES", [128, HPG, 128], 64), at("MS", [128, HPG, 128], 66), at("CS", [128, HPG, 128], 68)
    XD, XE = at("XD", [128, 256], 70), at("XE", [128, 256], 71)
    BT = at("BT", [128, 128], 72)
    HS, HT = at("HS", [128, 256], 73), at("HT", [128, 256], 74)
    AROW = at("AROW", [128, S], 75, F32R)
    SEL = at("SEL", [128, 8, 128], 79, F32R)
    MASKS = at("MASKS", [128, HPG, 128], 83, F32R)
    TDT, TAC, TDE = (at(n, [128, QB, 32], 85 + i) for i, n in enumerate(("TDT", "TAC", "TDE")))
    SQ2, RS2 = at("SQ2", [128, S], 88), at("RS2", [128, S], 92)
    SELF, MASKF = at("SELF", [128, 8, 128], 104), at("MASKF", [128, HPG, 128], 32)
    DZ, DE, DU, DL = (at(n, [128, S], 48 + 4 * i) for i, n in enumerate(("DZ", "DE", "DU", "DL")))
    DTT, ACS, EAC, DDE = (at(n, [128, S], kb) for n, kb in (("DTT", 88), ("ACS", 92), ("EAC", 96), ("DDE", 100)))
    RWH = [at("RWH0", [128, S], 40, F32R), at("RWH1", [128, S], 64, F32R)]
    RWL = [at("RWL0", [128, S], 44, F32R), at("RWL1", [128, S], 68, F32R)]
    assert W0 + 108 * K <= nc.sbuf_usable_end, (W0, nc.sbuf_usable_end)

    XSCR = nc.dram_tensor("xscr", (2, KT, 128, S), F32).ap()
    CSCR = nc.dram_tensor("cscr", (HEADS, 2, S), F32).ap()
    ASCR = nc.dram_tensor("ascr", (4, GROUPS * HPG, S), F32).ap()
    YSCR = nc.dram_tensor("yscr", (2 * KT, 128, S), F32).ap()

    PS = nc.alloc_psum_tensor("PS", [128, 8 * HALF], F32)

    def bank(b, n=1):
        return PS[:, b * HALF:(b + n) * HALF]

    def pp(slot):
        return bank(2 * slot, 2)

    SEM = {}

    def sem(name):
        if name not in SEM:
            SEM[name] = nc.alloc_semaphore(name)
        return SEM[name]

    raw_in = [sem("raw_in0"), sem("raw_in1")]
    w_split = sem("w_split")
    pp_full = sem("pp_full")
    pp_free = sem("pp_free")
    xsp0 = [sem("xspill0_even"), sem("xspill0_odd")]
    ada_in, ada_done, ada_ps, ada_ev = sem("ada_in"), sem("ada_done"), sem("ada_ps"), sem("ada_ev")
    w_pan = [w.rearrange("(k p) n -> p k n", p=128) for w in (fox_w_in[0], fox_w_o[0], ssm_w_in[0], ssm_w_out[0])]
    FOXW, WOW, SSMW, SOUTW = w_pan
    W1W = [mlp_w1[i].rearrange("(k p) n -> p k n", p=128) for i in range(2)]
    W2W = [mlp_w2[i].rearrange("(k p) n -> p k n", p=128) for i in range(2)]
    ADAW = [ada_w[i].rearrange("(k p) n -> p k n", p=128) for i in range(2)]

    with nc.Block() as block:
        @block.sync
        def _(sp):
            sp.dma_start(VIN[0:96, 0, :], ada_b.rearrange("l (r q) -> (l r) q", q=128)).then_inc(sem("vin"), 16)
            sp.dma_start(VIN[96:104, 0, :], c.rearrange("a (r q) -> (a r) q", q=128)).then_inc(sem("vin"), 16)
            for n, v in enumerate((ln_mix_g, ln_mix_b, ln_mlp_g, ln_mlp_b)):
                sp.dma_start(VIN[16 * n:16 * n + 16, 1, :], v.rearrange("l (r q) -> (l r) q", q=128)).then_inc(sem("vin"), 16)
            sp.dma_start(VIN[64:96, 1, :], ssm_conv_b.rearrange("a (r q) -> (a r) q", q=128)).then_inc(sem("vin"), 16)
            sp.dma_start(VIN[96:112, 1, :], ssm_norm_w.rearrange("a (r q) -> (a r) q", q=128)).then_inc(sem("vin"), 16)
            sp.dma_start(VIN[:, 2, :], ssm_conv_w[0].rearrange("t (r q) -> (t r) q", q=128)).then_inc(sem("vin"), 16)
            for k in range(KT):
                sp.dma_start(ADA0[:, k, :], ADAW[0][:, k, 0:2 * D]).then_inc(sem(f"ada0_{k}"), 16)
            xt = x[0].rearrange("(t p) d -> p t d", p=128)
            for h in range(2):
                sp.dma_start(XIN[:, 4 * h:4 * h + 4, :], xt[:, 4 * h:4 * h + 4, :]).then_inc(sem(f"xin{h}"), 16)
            sp.dma_start(DALL[:], ssm_d[0:1, :].partition_broadcast(128).rearrange("p a n -> p (a n)")).then_inc(sem("small_in"), 16)
            sp.wait_ge(sem("small_z"), 1)
            sp.dma_start(SMALL[112:128, 0:1], fox_b_f.rearrange("a h -> h a")).then_inc(sem("small_in"), 16)
            sp.dma_start(SMALL[96:128, 1:2], ssm_dt_bias.rearrange("a h -> h a")).then_inc(sem("small_in"), 16)
            sp.dma_start(SMALL[96:128, 2:3], ssm_a_log.rearrange("a h -> h a")).then_inc(sem("small_in"), 16)

            def load(P, par, src):
                if not (isinstance(P, int) and P < 2):
                    sp.wait_ge(w_split, P - 1)
                    sp.sem_inc(sem("load_go"), 1)
                sp.dma_start(RAW[:, par], src).then_inc(raw_in[par], 16)

            def load_ada(n, layer, col):
                if not (isinstance(n, int) and n == 0):
                    sp.wait_ge(ada_done, n)
                sp.dma_start(ADARAW[:], ADAW[layer][:, :, ds(col, 128)]).then_inc(ada_in, 16)

            load(0, 0, FOXW[:, :, 3 * D + HEADS - 128:3 * D + HEADS])
            for j in range(3):
                load(1 + j, (1 + j) % 2, FOXW[:, :, j * D:j * D + 128])
                load_ada(j, 0, (16 + j) * 128)
            for j in range(3):
                load(4 + j, j % 2, FOXW[:, :, j * D + 128:j * D + 256])
                load_ada(3 + j, 0, (19 + j) * 128)
            with sp.Fori(0, 3) as r:
                for k in range(6):
                    load(7 + 6 * r + k, (7 + k) % 2, FOXW[:, :, ds(256 * r + (k % 3) * D + (2 + k // 3) * 128, 128)])
                    load_ada(6 + 6 * r + k, 0, 768 * r + (22 + k) * 128)
            with sp.Fori(0, KT // 2) as r:
                for k in range(2):
                    load(P_WO + 2 * r + k, (P_WO + k) % 2, WOW[:, :, ds(256 * r + k * 128, 128)])
                    load_ada(24 + 2 * r + k, 0, 256 * r + (40 + k) * 128)

            def mlp(layer, P0, groups, ada):
                with sp.Fori(0, groups) as f:
                    with sp.Fori(0, KT // 2) as r:
                        for k in range(2):
                            load(P0 + 16 * f + 2 * r + k, (P0 + k) % 2, W1W[layer][:, :, ds(1024 * f + 256 * r + 128 * k, 128)])
                            if ada:
                                load_ada(32 + 16 * f + 2 * r + k, 1, 2048 * f + 256 * r + k * 128)
                    with sp.Fori(0, KT // 2) as r:
                        for k in range(2):
                            load(P0 + 16 * f + 8 + 2 * r + k, (P0 + k) % 2, W2W[layer][:, ds(8 * f, 8), ds(256 * r + 128 * k, 128)])
                            if ada:
                                load_ada(40 + 16 * f + 2 * r + k, 1, 2048 * f + 1024 + 256 * r + k * 128)

            def mlp_last(layer, P0):
                for st, (w, k0) in enumerate(((W1W[layer], 0), (W2W[layer], 24))):
                    with sp.Fori(0, KT // 2) as r:
                        for k in range(2):
                            col = 256 * r + 128 * k + (3072 if st == 0 else 0)
                            load(P0 + 48 + 8 * st + 2 * r + k, (P0 + k) % 2, w[:, k0:k0 + 8, ds(col, 128)])

            mlp(0, P_MLP0, 3, True)
            mlp_last(0, P_MLP0)
            load(P_DT, P_DT % 2, SSMW[:, :, DT0 + 32 - 128:DT0 + 32])

            def load_ssm(g, j):
                c0, step = ((2 * DI, 128), (2 * DI + D, 128), (DI, 256), (DI + 128, 256), (0, 256), (128, 256))[j]
                load(P_SSM + 6 * g + j, (P_SSM + j) % 2, SSMW[:, :, ds(step * g + c0, 128)])

            def store_y(g, par):
                for t in range(2):
                    sp.wait_ge(sem("yfin"), 2 * g + (t + 1))
                    sp.dma_start(YSCR[ds(2 * g + t, 1)].rearrange("a p n -> p a n"), YR[:, par, t:t + 1]).then_inc(sem("yout"), 16)

            for g in range(2):
                for j in range(6):
                    load_ssm(g, j)
            with sp.Fori(0, 3) as r:
                for q in range(2):
                    for j in range(6):
                        if j == 4:
                            store_y(2 * r + q, q)
                        load_ssm(2 * r + (2 + q), j)

            def load_out(f, m, k):
                load(P_OUT + 8 * f + m, (P_OUT + k) % 2, SOUTW[:, 8 * f:8 * f + 8, ds(128 * m, 128)])

            for m in range(4):
                load_out(0, m, m % 2)
            store_y(6, 0)
            store_y(7, 1)
            for f in range(2):
                with sp.Fori(2 - 2 * f, KT // 2) as r:
                    for k in range(2):
                        load_out(f, 2 * r + k, k)
            mlp(1, P_MLP1, 3, False)
            mlp_last(1, P_MLP1)

        @block.gpsimd
        def _(pool):
            ch = Count(sem("pool_c"))

            def do(ins):
                ch.inc(ins)
                pool.wait_ge(ch.sem, ch.n)

            do(pool.memset(IDF[:], 0.0))
            do(pool.affine_select(out=IDF[:], in_=IDF[:], compare_op=ALU.not_equal, fill=1.0, base=0,
                                  pattern=[[-1, 128]], channel_multiplier=1))
            pool.memset(ONESF[:], 1.0).then_inc(sem("consts"), 1)
            do(pool.tensor_scalar(IDR[:], IDF[:], 1.0, 1.0, ALU.mult, ALU.mult))
            do(pool.memset(ADAACC[:, 0, :], 0.0))
            do(pool.affine_select(out=ADAACC[:, 0, :], in_=ADAACC[:, 0, :], compare_op=ALU.is_ge, fill=MASKED, base=0,
                                  pattern=[[-1, 128]], channel_multiplier=1))
            do(pool.tensor_scalar(MASKA[:], ADAACC[:, 0, :], 1.0, 1.0, ALU.mult, ALU.mult))
            do(pool.memset(ONES2[:].bitcast(F32), 0.0))
            do(pool.memset(ONES2[0:2, :].bitcast(F32), 1.0))
            do(pool.memset(ONES2[64:66, :].bitcast(F32), 1.0))
            pool.wait_ge(sem("vec_ps"), 1)
            pool.memset(NCR[:].bitcast(F32), 0.0).then_inc(sem("consts"), 1)
            pool.sem_inc(sem("whi"), 1)

            def split(P, par, used):
                pool.wait_ge(raw_in[par], 16 * ((P - par) // 2 + 1) if isinstance(P, int) else used[1])
                if used[0] is not None:
                    pool.wait_ge(pp_full, used[0])
                pool.sem_inc(sem("split_go"), 1)
                pool.tensor_scalar(WH[:, par], RAW[:, par], 1.0, 1.0, ALU.mult, ALU.mult).then_inc(sem("whi"), 1)
                pool.wait_ge(sem("whi"), P + 2)
                pool.tensor_tensor(WL[:, par], RAW[:, par], WH[:, par].bitcast(F32), ALU.subtract).then_inc(w_split, 1)

            def panel(P, par, U2):
                split(P, par, (U2, 8 * P + (16 - 8 * par)))

            cond = COND[:, 0:8].unsqueeze(2).broadcast_to([128, KT, 128])

            def ada(n, slot):
                pool.wait_ge(ada_in, 16 * n + 16)
                pool.wait_ge(ada_ev, n + 1)
                s = sem("ada_c")
                v = ADARAW[:]
                steps = [lambda: pool.tensor_tensor(v, v, cond, ALU.mult),
                         lambda: pool.tensor_tensor(v[:, 0:4], v[:, 0:4], v[:, 4:8], ALU.add),
                         lambda: pool.tensor_tensor(v[:, 0:2], v[:, 0:2], v[:, 2:4], ALU.add)]
                for i, f in enumerate(steps):
                    f().then_inc(s, 1)
                    pool.wait_ge(s, 3 * n + i + 1)
                pool.tensor_tensor(ADAACC[:, slot], v[:, 0], v[:, 1], ALU.add).then_inc(ada_done, 1)

            panel(0, 0, None)
            panel(1, 1, None)
            pool.wait_ge(sem("cond"), 1)
            ada(0, 0)
            panel(2, 0, U_F + 1)
            ada(1, 1)
            with pool.Fori(0, 4) as r:
                r8 = 8 * r
                for k in range(6):
                    panel(6 * r + (3 + k), (3 + k) % 2, r8 + (U_FOX + 4 * (k // 3) + k % 3 + 1))
                    ada(6 * r + (2 + k), k % 2)

            def to_u(m, src):
                pool.tensor_scalar(UH[:, m], src[:, m], 1.0, 1.0, ALU.mult, ALU.mult).then_inc(sem("uhp"), 1)

            pool.wait_ge(pp_full, U_WO - 1)
            for m in range(KT):
                pool.wait_ge(sem("pv_ev"), 8 * (m + 1) + 1)
                to_u(m, Y0)
                pool.wait_ge(sem("uhp"), m + 1)
                pool.tensor_tensor(UL[:, m], Y0[:, m], UH[:, m].bitcast(F32), ALU.subtract).then_inc(sem("ulp"), 1)
            def panels(P0, P1, ada_too=False):
                with pool.Fori(0, (P1 - P0) // 2) as r:
                    for k in range(2):
                        panel(2 * r + (P0 + k), (P0 + k) % 2, 2 * r + (P0 - 2 + k + U_OF_P + 1))
                        if ada_too:
                            ada(2 * r + (P0 - 1 + k), (P0 - 1 + k) % 2)

            def low(n):
                for h in range(2):
                    v = slice(h * HALF, (h + 1) * HALF)
                    for k in range(KT):
                        pool.wait_ge(sem("uh"), 8 + 16 * n + 8 * h + k + 1)
                        pool.tensor_tensor(UL[:, k, v], U32[:, k % 2], UH[:, k, v].bitcast(F32), ALU.subtract).then_inc(sem("ul"), 1)

            panels(27, P_MLP0 + 2, True)
            low(0)
            panels(P_MLP0 + 2, P_MLP0 + 48, True)
            panels(P_MLP0 + 48, P_DT + 2)
            low(1)
            for P in (P_SSM + 1, P_SSM + 2):
                panel(P, P % 2, P - 2 + U_OF_P + 1)
            ch2 = Count(sem("pool_c2"))

            def do2(ins):
                ch2.inc(ins)
                pool.wait_ge(ch2.sem, ch2.n)

            pool.wait_ge(sem("xspill1"), 16 * KT)
            do2(pool.memset(SELF[:], 0.0))
            sv = SELF[:].rearrange("p (a h) n -> p a h n", a=2)
            for b in (0, -4):
                do2(pool.affine_select(out=sv, in_=sv, compare_op=ALU.not_equal, fill=1.0, base=b,
                                       pattern=[[-8, 2], [-1, 4], [0, 128]], channel_multiplier=1))
            do2(pool.tensor_scalar(SEL[:], SELF[:], 1.0, 1.0, ALU.mult, ALU.mult))
            do2(pool.memset(MASKF[:], 0.0))
            do2(pool.affine_select(out=MASKF[:], in_=MASKF[:], compare_op=ALU.is_ge, fill=MASKED, base=0,
                                   pattern=[[0, 4], [1, 128]], channel_multiplier=-1))
            do2(pool.tensor_scalar(MASKS[:], MASKF[:], 1.0, 1.0, ALU.mult, ALU.mult))
            pool.memset(AROW[:].bitcast(F32), 0.0).then_inc(sem("ssm_consts"), 1)
            panels(P_SSM + 3, P_OUT + 1)
            panel(P_OUT + 1, (P_OUT + 1) % 2, P_OUT - 1 + U_OF_P + 1)
            for m in range(KT):
                pool.wait_ge(sem(f"y0_in{m}"), 16)
                to_u(m, Y0)
                pool.wait_ge(sem("uhp"), KT + m + 1)
                pool.tensor_tensor(UL[:, m], Y0[:, m], UH[:, m].bitcast(F32), ALU.subtract).then_inc(sem("ulp"), 1)
            for m in range(2, 8):
                P = P_OUT + m
                panel(P, P % 2, P - 2 + U_OF_P + 1)
                for i in range(2 * m - 8, 2 * m - 6) if m >= 4 else ():
                    pool.wait_ge(sem(f"y1_in{i}"), 16)
                    pool.wait_ge(sem("ulp"), 2 * KT)
                    pool.tensor_scalar(HH[:, i], Y1[:, i], 1.0, 1.0, ALU.mult, ALU.mult).then_inc(sem("hhp"), 1)
                    pool.wait_ge(sem("hhp"), i + 1)
                    pool.tensor_tensor(HL[:, i], Y1[:, i], HH[:, i].bitcast(F32), ALU.subtract).then_inc(sem("hlp"), 1)
            panels(P_OUT + 8, P_MLP1 + 2)
            low(2)
            panels(P_MLP1 + 2, P_END)

        @block.tensor
        def _(pe):
            def panel(slot, par, xh, xl, lo=0, hi=48, wait_k=None):
                P_ = pp(slot)
                for n in range(lo, hi):
                    k, j = divmod(n, 6)
                    if j == 0 and wait_k is not None:
                        wait_k(k)
                    w, v, h = ((WH, xh, 0), (WH, xh, 1), (WH, xl, 0), (WH, xl, 1), (WL, xh, 0), (WL, xh, 1))[j]
                    mm = pe.matmul(P_[:, h * HALF:(h + 1) * HALF], w[:, par, k, :], v[:, k, h * HALF:(h + 1) * HALF],
                                   start=(k == 0 and j < 2), stop=(k == KT - 1 and j >= 4))
                return mm

            def begin(P, U, ahead=1):
                pe.wait_ge(w_split, P + 1)
                pe.wait_ge(pp_free, U + ahead)

            def two_panels(P, ul0):
                for k in range(2):
                    begin(P + k, P + k + U_OF_P)
                for h in range(2):
                    v = slice(h * HALF, (h + 1) * HALF)
                    for i in range(KT):
                        pe.wait_ge(sem("uh"), ul0 + 8 * h + i + 1)
                        for n, (w, m) in enumerate(((WH, UH), (WL, UH), (WH, UL))):
                            if n == 2:
                                pe.wait_ge(sem("ul"), ul0 + 8 * h + i + 1)
                            for k in range(2):
                                mm = pe.matmul(pp((P + k + U_OF_P) % 2)[:, v], w[:, (P + k) % 2, i, :], m[:, i, v],
                                               start=(i == 0 and n == 0), stop=(i == KT - 1 and n == 2))
                                if h == 1 and i == KT - 1 and n == 2:
                                    mm.then_inc(pp_full, 1)

            def ada(n, slot):
                pe.wait_ge(ada_done, n + 1)
                pe.wait_ge(ada_ev, n + 2)
                pe.matmul(bank(7)[:, 0:1], ADAACC[:, slot], ONESF[:, 0:1], start=True, stop=True).then_inc(ada_ps, 1)

            pe.wait_ge(sem("pool_c"), 2)
            pe.wait_ge(sem("vin"), 16 * 9)
            for n, rows in enumerate((104, 112, 128)):
                mm = pe.transpose(bank(4)[:, 128 * n:128 * n + rows], VIN[0:rows, n, :], IDF[0:rows, 0:rows])
            mm.then_inc(sem("vec_ps"), 1)
            pe.wait_ge(sem("cond"), 1)
            for k in range(KT):
                pe.wait_ge(sem(f"ada0_{k}"), 16)
                for j in range(16):
                    mm = pe.matmul(bank(5)[:, j:j + 1], ADA0[:, k, j * 128:(j + 1) * 128], COND[:, k:k + 1],
                                   start=(k == 0 and j == 0), stop=(k == KT - 1), skip_group_check=True)
            mm.then_inc(sem("ada0_ps"), 1)
            pe.wait_ge(sem("xin0"), 16)
            pe.wait_ge(sem("xin1"), 16)
            for k in range(KT):
                pe.wait_ge(pp_free, k + 1)
                for t in range(QB):
                    mm = pe.transpose(pp(k % 2)[:, t * 128:(t + 1) * 128], XIN[:, t, k * 128:(k + 1) * 128], IDF[:])
                mm.then_inc(pp_full, 1)
            begin(0, U_F)
            panel(0, 0, UH, UL, wait_k=lambda k: pe.wait_ge(sem("ul"), k + 1)).then_inc(pp_full, 1)

            def fox(it, par, panels, attend):
                a = it - 1
                pb, ab = par, 1 - par
                p0 = 1 + par
                u0 = 4 * it + U_FOX

                def filler(n):
                    j, i = divmod(n, 11)
                    if panels and n == 33:
                        pe.wait_ge(pp_free, u0 + (3 + 2))
                        for b in range(QB):
                            mm = pe.transpose(pp(0)[:, 128 * b:128 * b + 128], VT[:, 128 * b:128 * b + 128], IDF[:])
                        mm.then_inc(pp_full, 1)
                    if not panels or i == 10 or n >= 33:
                        return
                    lo, hi = 48 * i // 10, 48 * (i + 1) // 10
                    if i == 0:
                        begin(3 * it + (P_FOX + j), u0 + j, 2)
                    mm = panel(0, (p0 + j) % 2, UH, UL, lo, hi)
                    if hi == 48:
                        mm.then_inc(pp_full, 1)
                        ada(3 * it + j, (par + j) % 2)

                def scores(t):
                    s, i = divmod(t, QB)
                    rows = slice(64 * s, 64 * s + 64)
                    n = 128 * (i + 1)
                    pe.wait_ge(sem("exp"), 16 * a + (t + 1))
                    for lo in range(0, n, HALF):
                        w = min(HALF, n - lo)
                        o = bank(2, 2)[:, lo:lo + w]
                        q, kk = slice(128 * i, 128 * i + 128), slice(lo, lo + w)
                        diag = lo + w == n
                        pe.matmul(o, QH[rows, ab, q], KH[rows, ab, kk], start=True, stop=False)
                        pe.matmul(o, QH[rows, ab, q], KL[rows, ab, kk], start=False, stop=False)
                        pe.matmul(o, QL[rows, ab, q], KH[rows, ab, kk], start=False, stop=False)
                        if diag:
                            pe.matmul(bank(2, 2)[:, n - 128:n], IDR[:], MASKA[:], start=False, stop=False, skip_group_check=True)
                        mm = pe.matmul(o, ONES2[rows, :], NCR[rows, kk], start=False, stop=True)
                    mm.then_inc(sem("sc"), 1)

                def turn(t, b):
                    s, i = divmod(t, QB)
                    u = 12 * s + [0, 1, 2, 3, 4, 6, 8, 10][i] + b
                    if b == 0:
                        pe.wait_ge(sem("p"), 16 * a + (t + 2))
                        pe.wait_ge(sem("ptl"), 24 * a + (u + 1))
                    for j in range(4 * b, min(4 * b + 4, i + 1)):
                        mm = pe.transpose(bank(4 + b)[:, 128 * (j % 4):128 * (j % 4) + 128], PN[:, t % 2, 128 * j:128 * j + 128], IDF[:])
                    mm.then_inc(sem("pt"), 1)

                def pv(t):
                    s, i = divmod(t, QB)
                    u = 12 * s + [0, 1, 2, 3, 4, 6, 8, 10][i] + (i >= 4)
                    pe.wait_ge(sem("ptl"), 24 * a + (u + 2))
                    if i % 2 == 0:
                        pe.wait_ge(sem("pv_ev"), 8 * a + (t // 2 + 1))
                    o = bank(6)[:, 256 * (i % 2):256 * (i % 2) + 256]
                    for j in range(i + 1):
                        mm = pe.matmul(o, VV[:, ab, j, s].rearrange("p a d -> p (a d)"), PT[:, j].rearrange("p a q -> p (a q)"),
                                       start=(j == 0), stop=(j == i))
                    mm.then_inc(sem("pv"), 1)

                if attend:
                    pe.wait_ge(sem("ncr_in"), 32 * a + 32)
                    pe.wait_ge(pp_free, 4 * a + (U_FOX + 4))
                for t in range(18):
                    if attend:
                        if t < 16:
                            scores(t)
                        if t == 2:
                            pe.wait_ge(pp_free, 4 * a + (U_FOX + 6))
                        if t >= 2:
                            pv(t - 2)
                        if 1 <= t <= 16:
                            turn(t - 1, 0)
                    filler(2 * t)
                    if attend and 1 <= t <= 16 and (t - 1) % QB >= 4:
                        turn(t - 1, 1)
                    filler(2 * t + 1)

            rounds(pe, fox)

            def stats(n):
                pe.wait_ge(sem("sqd"), 7 * (n + 1))
                for q, v in enumerate((TA, TB)):
                    for h in range(2):
                        mm = pe.matmul(bank(4 + 2 * q + h), ONESF[:], v[:, h * HALF:(h + 1) * HALF], start=True, stop=True)
                mm.then_inc(sem("stats"), 1)

            with pe.Fori(0, KT // 2) as r:
                for k in range(2):
                    P = P_WO + k
                    begin(2 * r + P, 2 * r + (P + U_OF_P), 1)
                    panel((P + U_OF_P) % 2, P % 2, UH, UL, wait_k=(lambda i: pe.wait_ge(sem("ulp"), i + 1)) if k == 0 else None).then_inc(pp_full, 1)
                    ada(2 * r + (24 + k), k % 2)
            pe.wait_ge(ada_ev, 32 + 2)
            stats(0)

            def mlp(layer, P0, ul0):
                def one(off, expr, k, xh, xl, ada_too, wait_k=None):
                    P = P0 + off + k
                    begin(expr + P, expr + (P + U_OF_P), 1)
                    panel((P + U_OF_P) % 2, P % 2, xh, xl, wait_k=wait_k).then_inc(pp_full, 1)
                    if ada_too:
                        ada(expr + (32 + off + k), k)

                def first(ada_too, f):
                    two_panels(P0, ul0)
                    for k in range(2):
                        if ada_too:
                            ada(32 + k, k)
                    with pe.Fori(0, KT // 2 - 1) as r:
                        for k in range(2):
                            one(2, 2 * r, k, UH, UL, ada_too)

                def second(ada_too, f):
                    with pe.Fori(0, KT // 2) as r:
                        for k in range(2):
                            one(8, 16 * f + 2 * r, k, HH, HL, ada_too,
                                wait_k=(lambda i: pe.wait_ge(sem("hl"), 8 * f + (32 * layer + i + 3))) if k == 0 else None)

                ada_too = layer == 0
                first(ada_too, 0)
                second(ada_too, 0)
                with pe.Fori(1, 3) as f:
                    with pe.Fori(0, KT // 2) as r:
                        for k in range(2):
                            one(0, 16 * f + 2 * r, k, UH, UL, ada_too)
                    second(ada_too, f)
                with pe.Fori(0, KT // 2) as r:
                    for k in range(2):
                        one(48, 2 * r, k, UH, UL, False)
                second(False, 3)

            mlp(0, P_MLP0, 8)
            pe.wait_ge(ada_ev, ADA_JOBS + 2)
            stats(1)
            two_panels(P_DT, 24)

            def ssm(it, par, panels, scan):
                g = it - 1
                xs, bc = XS[1 - par], BC[1 - par]
                SG, EB, TR, YB = bank(4), bank(5), bank(6), bank(7)

                def filler(piece, lo, hi):
                    if not panels:
                        i = piece - 4
                        a, b = 8 * i, 8 * i + 8
                        for k in range(2):
                            a_, b_ = max(a, 48 * k), min(b, 48 * k + 48)
                            if 0 <= a_ < b_:
                                if a_ == 48 * k:
                                    begin(P_OUT + k, P_OUT + k + U_OF_P)
                                mm = panel((P_OUT + k + U_OF_P) % 2, (P_OUT + k) % 2, UH, UL, a_ - 48 * k, b_ - 48 * k,
                                           wait_k=(lambda t: pe.wait_ge(sem("ulp"), KT + t + 1)) if k == 0 else None)
                                if b_ == 48 * k + 48:
                                    mm.then_inc(pp_full, 1)
                        return
                    for j in range(0 if scan else 1, 6):
                        a, b = max(lo, 48 * j), min(hi, 48 * j + 48)
                        if a < b:
                            P = P_SSM + j
                            if a == 48 * j:
                                begin(6 * it + P, 6 * it + (P + U_OF_P), 1)
                            mm = panel((P + U_OF_P) % 2, P % 2, UH, UL, a - 48 * j, b - 48 * j)
                            if b == 48 * j + 48:
                                mm.then_inc(pp_full, 1)

                for cnk in range(QB):
                    if scan:
                        l = slice(128 * cnk, 128 * cnk + 128)
                        if cnk == 0:
                            pe.wait_ge(sem("arow_in"), 64 * g + 64)
                            pe.wait_ge(sem("silu"), 6 * g + 5)
                            pe.wait_ge(sem("tables"), 3)
                            pe.wait_ge(sem("rms_ev"), g + 1)
                        pe.wait_ge(sem("hs"), 8 * g + (cnk + 1))
                        for h in range(HPG):
                            pe.matmul(SG[:, 128 * h:128 * h + 128], SEL[:, h], AROW[:, l], start=(h == 0), stop=False, skip_group_check=True)
                        mm = pe.matmul(SG, IDR[:], MASKS[:].rearrange("p h n -> p (h n)"), start=False, stop=True, skip_group_check=True)
                        mm.then_inc(sem("sg"), 1)
                        for h in range(HPG):
                            mm = pe.matmul(EB[:, 128 * h:128 * h + 128], SEL[:, 4 + h], AROW[:, l], start=True, stop=True)
                        mm.then_inc(sem("eb"), 1)
                        pe.wait_ge(sem("ms"), 8 * g + (cnk + 1))
                        pe.transpose(TR[:, 0:128], xs[:, 0, l], IDF[:])
                        pe.transpose(TR[:, 128:256], xs[:, 1, l], IDF[:])
                        pe.transpose(TR[:, 256:384], bc[:, 0, l], IDF[:])
                        pe.matmul(TR[:, 384:512], bc[:, 0, l], bc[:, 1, l], start=True, stop=True).then_inc(sem("tr"), 1)
                    filler(2 * cnk, 36 * cnk, 36 * cnk + 14)
                    if scan:
                        pe.wait_ge(sem("ms"), 8 * g + (cnk + 2))
                        pe.wait_ge(sem("yev"), 8 * g + (cnk + 1))
                        for h in range(HPG):
                            o, t = YB[:, 128 * h:128 * h + 128], slice(128 * (h // 2), 128 * (h // 2) + 128)
                            pe.matmul(o, XD[:, t], MS[:, h], start=True, stop=False)
                            mm = pe.matmul(o, HS[:, t], CS[:, h], start=False, stop=True)
                        mm.then_inc(sem("yps"), 1)
                        if cnk < QB - 1:
                            pe.matmul(SG[:, 0:256], BT[:], XE[:], start=True, stop=True).then_inc(sem("st"), 1)
                    filler(2 * cnk + 1, 36 * cnk + 14, 36 * cnk + 36)
                if scan:
                    pe.wait_ge(sem("ysq"), g + 1)
                    pe.wait_ge(sem("hs"), 8 * g + 9)
                    for h in range(2):
                        mm = pe.matmul(bank(4 + h), ONESF[:], SQ2[:, h * HALF:(h + 1) * HALF], start=True, stop=True)
                    mm.then_inc(sem("rms"), 1)
                else:
                    pe.wait_ge(sem("dtrows"), 1)
                    for q, v in enumerate((DTT, ACS, DDE)):
                        for j in range(QB):
                            mm = pe.transpose(bank(4, 2)[:, 256 * q + 32 * j:256 * q + 32 * j + 32],
                                              v[96:128, 128 * j:128 * j + 128], IDF[96:128, 96:128])
                    mm.then_inc(sem("tab_ps"), 1)

            rounds(pe, ssm)
            for f, (xh, xl) in enumerate(((UH, UL), (HH, HL))):
                with pe.Fori(1 - f, KT // 2) as r:
                    for k in range(2):
                        P = P_OUT + 8 * f + k
                        begin(2 * r + P, 2 * r + (P + U_OF_P), 1)
                        panel((P + U_OF_P) % 2, P % 2, xh, xl,
                              wait_k=(lambda i: pe.wait_ge(sem("hlp"), i + 1)) if f == 1 and k == 0 else None).then_inc(pp_full, 1)
            stats(2)
            mlp(1, P_MLP1, 40)
            stats(3)
            for t in range(QB):
                if t % 4 == 0:
                    pe.wait_ge(sem("rfin"), KT * (t // 4 + 1))
                pe.wait_ge(pp_free, U_END + t + 1)
                for k in range(KT):
                    mm = pe.transpose(pp((U_END + t) % 2)[:, k * 128:(k + 1) * 128], R[:, k, t * 128:(t + 1) * 128], IDF[:])
                mm.then_inc(pp_full, 1)


        def v_flat(ps):
            return ps.rearrange("p (b d) -> p b d", d=DH)

        def v_part(par, part):
            return VV[:, par].rearrange("p j s c d -> p (j s) c d")[:, :, part]

        def uses(t):
            s, i = divmod(t, QB)
            return 12 * s + [0, 1, 2, 3, 4, 6, 8, 10][i]

        TAKEN = {4: 0, 10: 1, 15: 2, 17: 3}
        EVICT = {2: 0, 3: 1, 4: 2, 6: 3, 7: 4}

        @block.scalar
        def _(act):
            own = Count(sem("act_c"))

            def link(ins):
                own.inc(ins)
                act.wait_ge(own.sem, own.n)

            act.sem_inc(sem("exp"), 1)
            act.sem_inc(sem("pv_ev"), 1)
            act.sem_inc(sem("yout"), 32)
            act.wait_ge(sem("vecs"), 4)
            act.activation(COND[:, 8:16], COND[:, 8:16], ACT.Tanh).then_inc(sem("condt"), 1)
            act.wait_ge(sem("mod0"), 2)
            for k in range(KT):
                act.wait_ge(pp_full, k + 1)
                if k >= 2:
                    act.wait_ge(sem("ul"), k - 1)
                    act.wait_ge(xsp0[k % 2], 16 * (k // 2))
                ps = pp(k % 2)
                link(act.activation(XU[:, k % 2], ps, ACT.Identity, bias=MOD[:, k:k + 1], scale=COLS[:, 3, 0, k:k + 1]))
                act.activation(RST[:, k % 2], ps, ACT.Copy, scale=ALPHA).then_inc(pp_free, 1)
                act.activation(UH[:, k], XU[:, k % 2], ACT.Copy).then_inc(sem("uh"), 1)
                act.wait_ge(sem("uh"), k + 1)
                act.dma_start(XSCR[0, k], RST[:, k % 2]).then_inc(xsp0[k % 2], 16)

            q96 = slice(96, 128)

            def log1p_exp(n, m, e, u, l):
                act.wait_ge(sem("sp_m"), n + 1)
                act.activation(e[q96], m[q96], ACT.Exp, scale=-1.0).then_inc(sem("sp_e"), 1)
                act.wait_ge(sem("sp_u"), n + 1)
                link(act.activation(l[q96], u[q96], ACT.Ln))
                act.wait_ge(sem("sp_r"), n + 1)
                act.activation(u[q96], l[q96], ACT.Exp, scale=-1.0).then_inc(sem("sp_l"), 1)

            log1p_exp(0, FM, FE, FU, FL)
            def load_ncr(pair):
                for s in range(2):
                    src = CSCR[ds(2 * pair + s, 1)].rearrange("a b n -> (a b) n")
                    act.dma_start(NCR[64 * s:64 * s + 2, :].bitcast(F32), src).then_inc(sem("ncr_in"), 16)

            def cumulated():
                act.wait_ge(sem("fcum"), 1)
                act.activation(FNH[q96], FC[q96], ACT.Copy).then_inc(sem("fnh"), 1)
                act.wait_ge(sem("fnh"), 1)
                act.dma_start(CSCR[:, 0, :], FNH[112:128, :].bitcast(F32)).then_inc(sem("cscr"), 16)
                act.wait_ge(sem("fnl"), 1)
                act.dma_start(CSCR[:, 1, :], FNL[112:128, :].bitcast(F32)).then_inc(sem("cscr"), 16)
                act.wait_ge(sem("cscr"), 32)
                act.wait_ge(sem("consts"), 2)
                load_ncr(0)

            def fox(it, par, panels, attend):
                a = it - 1
                u0 = 4 * it + U_FOX

                def take(j):
                    if j < 3:
                        act.wait_ge(pp_full, u0 + (j + 1))
                    if j == 2:
                        act.activation(VT[:], pp(0), ACT.Copy).then_inc(pp_free, 1)
                    elif j == 3:
                        act.wait_ge(pp_full, u0 + 4)
                        act.activation(v_part(par, 0), v_flat(pp(0)), ACT.Copy).then_inc(sem("qkvh"), 1)
                    else:
                        act.activation((QH, KH)[j][:, par], pp(0), ACT.Copy, scale=(DH ** -0.5, 1.0)[j]).then_inc(sem("qkvh"), 1)

                def hi(t, b):
                    nb = min(4, t % QB + 1 - 4 * b)
                    act.wait_ge(sem("pt"), 24 * a + (uses(t) + b + 1))
                    act.activation(PT[:, 4 * b:4 * b + nb, 0], bank(4 + b)[:, 0:128 * nb].rearrange("p (a b) -> p a b", b=128),
                                   ACT.Copy).then_inc(sem("pth"), 1)

                for t in range(18):
                    if attend:
                        if 1 <= t <= 16:
                            hi(t - 1, 0)
                        if t >= 2 and t % 2 == 1:
                            act.wait_ge(sem("pv"), 16 * a + (t - 1))
                            act.activation(OSUM[:].rearrange("p (b q) -> p b q", q=128),
                                           bank(6)[0:64].rearrange("p (b c q) -> p b c q", b=2, q=128)[:, :, 0],
                                           ACT.Copy).then_inc(sem("ocopy"), 1)
                        if t < 16:
                            n = 128 * (t % QB + 1)
                            act.wait_ge(sem("mx"), 16 * a + (t + 1))
                            act.wait_ge(sem("p"), 16 * a + (t + 1))
                            act.activation(PE_[:, 0:n], bank(2, 2)[:, 0:n], ACT.Exp, bias=NEGM[:, t % 2:t % 2 + 1],
                                           accum_out=RSUM[:, t % 2:t % 2 + 1]).then_inc(sem("exp"), 1)
                            if t == 15 and panels:
                                load_ncr(it)
                        if 1 <= t <= 16 and (t - 1) % QB >= 4:
                            hi(t - 1, 1)
                    if panels and t in TAKEN:
                        take(TAKEN[t])
                    if not attend and t == 4:
                        cumulated()

            rounds(act, fox)

            def reload(n, m0=0, m1=KT):
                for m in range(m0, m1):
                    act.dma_start(R[:, m], XSCR[n, m]).then_inc(sem(f"r_in{m}"), 16)

            def squares(n, U):
                for m in range(KT):
                    act.wait_ge(pp_free, U + m + 3)
                    if m == 0:
                        act.activation(TB[:], R[:, 0], ACT.Square).then_inc(sem("sqa"), 1)
                        continue
                    if 7 * n + m - 1 > 0:
                        act.wait_ge(sem("sqd"), 7 * n + m - 1)
                    act.activation(SQ[:], R[:, m], ACT.Square).then_inc(sem("sqa"), 1)

            outd = [sem("out_even"), sem("out_odd")]

            def result(t):
                act.wait_ge(pp_full, U_END + t + 1)
                if t >= 2:
                    act.wait_ge(outd[t % 2], 16 * (t // 2))
                act.activation(OST[:, t % 2], pp((U_END + t) % 2), ACT.Copy).then_inc(pp_free, 1)
                act.wait_ge(pp_free, U_END + t + 3)
                act.dma_start(out[0, 128 * t:128 * t + 128, :], OST[:, t % 2]).then_inc(outd[t % 2], 16)

            def norm(n, to_scratch=None, last=False):
                act.wait_ge(sem("stats"), n + 1)
                for h in range(2):
                    act.activation(LS[:, h * HALF:(h + 1) * HALF], bank(4 + h), ACT.Square, scale=1.0 / D).then_inc(sem("ls"), 1)
                for h in range(2):
                    v = slice(h * HALF, (h + 1) * HALF)
                    act.wait_ge(sem("lv"), 2 * n + h + 1)
                    link(act.activation(LV[:, v], LV[:, v], ACT.Ln))
                for h in range(2):
                    v = slice(h * HALF, (h + 1) * HALF)
                    act.activation(LA[:, v], LV[:, v], ACT.Exp, scale=-0.5).then_inc(sem("la"), 1)
                for h in range(2):
                    v = slice(h * HALF, (h + 1) * HALF)
                    for k in range(KT):
                        act.wait_ge(sem("xn"), 16 * n + 8 * h + k + 1)
                        if last:
                            if h == 1 and k % 2 == 0:
                                result(k // 2)
                            act.activation(R[:, k, v], R[:, k, v], ACT.Identity, bias=VEC2[:, 56 + k:57 + k],
                                           scale=VEC2[:, 40 + k:41 + k]).then_inc(sem("rfin"), 1)
                            continue
                        e = 8 * h + k
                        act.wait_ge(sem("ul"), 8 + 16 * n + e - 1)
                        link(act.activation(U32[:, k % 2], R[:, k, v], ACT.Identity, bias=COLS[:, n, 1, k:k + 1],
                                            scale=COLS[:, n, 0, k:k + 1]))
                        act.activation(UH[:, k, v], U32[:, k % 2], ACT.Copy).then_inc(sem("uh"), 1)
                if last:
                    return
                if to_scratch is not None:
                    for k in range(KT):
                        act.wait_ge(sem("rp"), 8 * n + k + 1)
                        act.dma_start(XSCR[to_scratch, k], R[:, k]).then_inc(sem("xspill1"), 16)

            act.wait_ge(sem("pv_ev"), 8 * PAIRS + 1)
            for q in xsp0:
                act.wait_ge(q, 8 * KT)
            reload(0)
            squares(0, U_WO)
            norm(0)

            def mlp_act(layer, U0):
                c0 = own.n
                with act.Fori(0, 4) as f:
                    with act.Fori(0, KT // 2) as r:
                        own.at(c0 + 8 * f + 2 * r)
                        for k in range(2):
                            U = 16 * f + 2 * r + (U0 + k)
                            T = (TA, TB)[k]
                            act.wait_ge(pp_full, U + 1)
                            act.wait_ge(pp_free, U + 2)
                            act.wait_ge(sem("hl"), 8 * f + 2 * r + (32 * layer + k + 1))
                            act.activation(T[:], pp((U0 + k) % 2), ACT.Relu).then_inc(pp_free, 1)
                            act.wait_ge(pp_free, U + 3)
                            link(act.activation(T[:], T[:], ACT.Square))
                            act.activation(HH[:, ds(2 * r + k, 1)], T[:].unsqueeze(1), ACT.Copy).then_inc(sem("hh"), 1)
                own.at(c0 + 32)

            mlp_act(0, P_MLP0 + U_OF_P)
            squares(1, P_DT - KT + U_OF_P)
            norm(1, to_scratch=1)

            def conv_in(it, j):
                U = 6 * it + (P_SSM + j + U_OF_P)
                act.wait_ge(pp_full, U + 1)
                act.wait_ge(pp_free, U + 2)
                act.wait_ge(sem("silu"), 6 * it + (j + 1))
                col = (it + 16, it + 24, 2 * it, 2 * it + 1)[j]
                act.activation(XP[:, 3:3 + S], pp((P_SSM + j + U_OF_P) % 2), ACT.Copy).then_inc(pp_free, 1)
                act.wait_ge(pp_free, U + 3)
                act.activation(CT[:], XP[:, 3:3 + S], ACT.Identity, bias=CBH[:, ds(col, 1)],
                               scale=VEC3[:, ds(col + 96, 1)]).then_inc(sem("ct"), 1)

            conv_in(0, 0)
            act.activation(SMALL[q96, 3:4], SMALL[q96, 2:3], ACT.Exp).then_inc(sem("alog"), 1)
            log1p_exp(1, DDE, DE, DU, DL)
            act.wait_ge(sem("acs"), 1)
            act.activation(EAC[q96], ACS[q96], ACT.Exp).then_inc(sem("eac"), 1)
            act.activation(DDE[q96], DDE[q96], ACT.Exp).then_inc(sem("dde"), 1)
            act.wait_ge(sem("eac"), 1)
            for n, src in enumerate((ACS, EAC)):
                act.activation(RWH[n][q96], src[q96], ACT.Copy).then_inc(sem("rwh"), 1)
            act.wait_ge(sem("rwl"), 2)
            act.wait_ge(sem("rwh"), 2)
            for n, t in enumerate((RWH[0], RWL[0], RWH[1], RWL[1])):
                act.dma_start(ASCR[n], t[q96].bitcast(F32)).then_inc(sem("ascr"), 16)

            def load_arow(g):
                for q in range(4):
                    act.dma_start(AROW[4 * q:4 * q + 4, :].bitcast(F32), ASCR[q, ds(4 * g, 4), :]).then_inc(sem("arow_in"), 16)

            def ssm(it, par, panels, scan):
                g = it - 1
                gp = 1 - par

                def take(j):
                    if j < 4:
                        if not (j == 0 and not scan):
                            conv_in(it, j)
                        act.wait_ge(sem("conv"), 4 * it + (j + 1))
                        act.activation(TT[:], CT[:], ACT.Tanh).then_inc(sem("tt"), 1)
                    else:
                        ps = pp((P_SSM + j + U_OF_P) % 2)
                        act.wait_ge(pp_full, 6 * it + (P_SSM + j + U_OF_P + 1))
                        act.wait_ge(sem("silu"), 6 * it + (j + 1))
                        act.activation(CT[:], ps, ACT.Copy, scale=0.5).then_inc(sem("zh"), 1)
                        act.activation(TT[:], ps, ACT.Tanh, scale=0.5).then_inc(pp_free, 1)

                def rstd(g_):
                    act.wait_ge(sem("rms_ev"), g_ + 2)
                    act.activation(RS2[:], RS2[:], ACT.Ln).then_inc(sem("rln"), 1)
                    act.wait_ge(sem("rln"), g_ + 1)
                    act.activation(RS2[:], RS2[:], ACT.Exp, scale=-0.5).then_inc(sem("rsa"), 1)

                if not panels:
                    act.wait_ge(sem("yout"), 32 * (GROUPS - 1))
                    act.wait_ge(sem("silu"), 6 * GROUPS + 1)
                    act.wait_ge(sem("yev"), 8 * (GROUPS - 1) + 1)
                    for m in range(KT):
                        act.dma_start(Y0[:, m], YSCR[m]).then_inc(sem(f"y0_in{m}"), 16)
                for cnk in range(QB):
                    if scan:
                        act.wait_ge(sem("tr"), 8 * g + (cnk + 1))
                        act.activation(BT[:], bank(6)[:, 256:384], ACT.Copy).then_inc(sem("bt"), 1)
                        act.wait_ge(sem("seg"), 8 * g + (cnk + 1))
                        act.activation(ES[:], ES[:], ACT.Exp).then_inc(sem("es"), 1)
                        if cnk == 0 and not (isinstance(it, int) and it == 1):
                            rstd(it - 2)
                    if panels and cnk in EVICT:
                        take(EVICT[cnk])
                if scan and panels:
                    act.wait_ge(sem("yps"), 8 * g + 8)
                    load_arow(it)
                if scan:
                    act.wait_ge(sem("yev"), 8 * g + 9)
                    act.activation(SQ2[:], YR[:, gp, 0], ACT.Square).then_inc(sem("ysa"), 1)
                    act.activation(RS2[:], YR[:, gp, 1], ACT.Square).then_inc(sem("ysa"), 1)
                if panels:
                    take(5)
                else:
                    rstd(g)
                if not scan:
                    act.wait_ge(sem("ascr"), 64)
                    act.wait_ge(sem("ssm_consts"), 1)
                    load_arow(0)

            rounds(act, ssm)
            act.wait_ge(sem("hs"), 8 * GROUPS + 1)
            reload(1, 0, 6)
            act.wait_ge(sem("yfin"), 2 * GROUPS)
            reload(1, 6, KT)
            act.wait_ge(sem("yout"), 32 + 32 * GROUPS)
            for m in range(KT):
                act.dma_start(Y1[:, m], YSCR[KT + m]).then_inc(sem(f"y1_in{m}"), 16)
            squares(2, P_MLP1 - KT + U_OF_P)
            norm(2)
            mlp_act(1, P_MLP1 + U_OF_P)
            squares(3, P_END - KT + U_OF_P)
            norm(3, last=True)
            for t in range(4, QB):
                result(t)
            for q in outd:
                act.wait_ge(q, 8 * QB)

        @block.vector
        def _(dve):
            own = Count(sem("dve_c"))

            def link(ins):
                own.inc(ins)
                dve.wait_ge(own.sem, own.n)

            dve.sem_inc(pp_free, 2)
            dve.sem_inc(ada_ev, 2)
            dve.sem_inc(sem("ptl"), 1)
            dve.sem_inc(sem("p"), 1)
            dve.sem_inc(sem("hl"), 2)
            for s in ("hs", "ms", "yev", "rms_ev", "silu"):
                dve.sem_inc(sem(s), 1)
            dve.memset(SMALL[:], 0.0).then_inc(sem("small_z"), 1)
            dve.wait_ge(sem("vec_ps"), 1)
            for n, v in enumerate((VEC1, VEC2, VEC3)):
                link(dve.tensor_copy(v[:], bank(4)[:, 128 * n:128 * n + v.shape[1]]))
            vecs = sem("vecs")
            dve.tensor_scalar(COND[:, 8:16], VEC1[:, 96:104], 0.5, None, ALU.mult).then_inc(vecs, 1)
            dve.tensor_scalar(VEC3[:], VEC3[:], 0.5, None, ALU.mult).then_inc(vecs, 1)
            dve.tensor_scalar(CBH[:], VEC2[:, 64:96], 0.5, None, ALU.mult).then_inc(vecs, 1)
            dve.tensor_scalar(COND[:, 0:8], VEC1[:, 96:104], 0.5, None, ALU.mult).then_inc(vecs, 1)
            dve.wait_ge(vecs, 4)
            dve.wait_ge(sem("condt"), 1)
            dve.scalar_tensor_tensor(out=COND[:, 0:8], in0=COND[:, 8:16], scalar=1.0, in1=COND[:, 0:8],
                                     op0=ALU.add, op1=ALU.mult).then_inc(sem("cond"), 1)
            dve.wait_ge(sem("small_in"), 64)
            for s in range(2):
                rows = slice(64 * s, 64 * s + 64)
                dve.tensor_copy(DCOL[rows], DALL[rows].rearrange("p (t s) -> p t s", s=2)[:, :, s]).then_inc(sem("dcol"), 1)
            dve.wait_ge(sem("ada0_ps"), 1)
            dve.tensor_tensor(MOD[:, 0:16], bank(5)[:, 0:16], VEC1[:, 0:16], ALU.add).then_inc(sem("mod0"), 1)
            dve.wait_ge(sem("mod0"), 1)
            dve.tensor_scalar(COLS[:, 3, 0], MOD[:, 8:16], 1.0, None, ALU.add).then_inc(sem("mod0"), 1)
            for k in range(KT):
                dve.wait_ge(sem("uh"), k + 1)
                dve.tensor_tensor(UL[:, k], XU[:, k % 2], UH[:, k].bitcast(F32), ALU.subtract).then_inc(sem("ul"), 1)

            q96 = slice(96, 128)

            def log1p_exp(n, z, m, e, u, l):
                dve.scalar_tensor_tensor(out=m[q96], in0=z[q96], scalar=-1.0, in1=z[q96], op0=ALU.mult, op1=ALU.max).then_inc(sem("sp_m"), 1)
                dve.wait_ge(sem("sp_e"), n + 1)
                dve.tensor_scalar(u[q96], e[q96], 1.0, None, ALU.add).then_inc(sem("sp_u"), 1)
                dve.wait_ge(sem("sp_u"), n + 1)
                dve.scalar_tensor_tensor(out=m[q96], in0=u[q96], scalar=-1.0, in1=e[q96], op0=ALU.add, op1=ALU.subtract).then_inc(sem("sp_r"), 1)
                dve.wait_ge(sem("sp_l"), n + 1)
                dve.wait_ge(sem("sp_r"), n + 1)
                link(dve.tensor_tensor(m[q96], m[q96], u[q96], ALU.mult))
                link(dve.tensor_tensor(l[q96], l[q96], m[q96], ALU.subtract))

            dve.wait_ge(pp_full, U_F + 1)
            dve.tensor_scalar(FZ[q96], pp(0)[q96], SMALL[q96, 0:1], None, ALU.add).then_inc(pp_free, 1)
            dve.wait_ge(pp_free, U_F + 3)
            for q in xsp0:
                dve.wait_ge(q, 8 * KT)
            log1p_exp(0, FZ, FM, FE, FU, FL)
            link(dve.tensor_scalar(FZ[q96], FZ[q96], -1.0, 0.0, ALU.mult, ALU.max))
            link(dve.tensor_tensor(FZ[q96], FZ[q96], FL[q96], ALU.add))
            link(dve.memset(FM[q96], 1.0))
            dve.tensor_tensor_scan(FC[q96], FM[q96], FZ[q96], 0.0, ALU.mult, ALU.add).then_inc(sem("fcum"), 1)

            def ada(n):
                dve.wait_ge(ada_ps, n + 1)
                dve.tensor_tensor(MOD[:, ds(n + 16, 1)], bank(7)[:, 0:1], VEC1[:, ds(n + 16, 1)], ALU.add).then_inc(ada_ev, 1)

            def fox(it, par, panels, attend):
                a = it - 1
                u0 = 4 * it + U_FOX

                def take(j):
                    if j == 2:
                        return
                    j = min(j, 2)
                    dve.wait_ge(sem("qkvh"), 3 * it + (j + 1))
                    if j == 0:
                        dve.scalar_tensor_tensor(out=QL[:, par], in0=pp(0), scalar=DH ** -0.5, in1=QH[:, par].bitcast(F32),
                                                 op0=ALU.mult, op1=ALU.subtract).then_inc(pp_free, 1)
                    elif j == 1:
                        dve.tensor_tensor(KL[:, par], pp(0), KH[:, par].bitcast(F32), ALU.subtract).then_inc(pp_free, 1)
                    else:
                        dve.tensor_tensor(v_part(par, 1), v_flat(pp(0)), v_part(par, 0).bitcast(F32), ALU.subtract).then_inc(pp_free, 1)
                    ada(3 * it + j)

                def lo(t, b):
                    nb = min(4, t % QB + 1 - 4 * b)
                    dve.wait_ge(sem("pth"), 24 * a + (uses(t) + b + 1))
                    dve.tensor_tensor(PT[:, 4 * b:4 * b + nb, 1], bank(4 + b)[:, 0:128 * nb].rearrange("p (a b) -> p a b", b=128),
                                      PT[:, 4 * b:4 * b + nb, 0].bitcast(F32), ALU.subtract).then_inc(sem("ptl"), 1)

                def output(t):
                    s, i = divmod(t, QB)
                    dve.wait_ge(sem("ocopy"), 8 * a + (t // 2 + 1))
                    o = bank(6).rearrange("p (b c q) -> p b c q", b=2, q=128)
                    tmp = OSUM[0:64].rearrange("p (b q) -> p b q", q=128)
                    e = 16 * a + 2 * (t // 2)
                    dve.tensor_tensor(tmp, tmp, o[0:64, :, 1], ALU.add).then_inc(sem("osum"), 1)
                    dve.wait_ge(sem("osum"), e + 1)
                    dve.tensor_tensor(tmp, tmp, o[64:128, :, 0], ALU.add).then_inc(sem("osum"), 1)
                    dve.wait_ge(sem("osum"), e + 2)
                    dst = Y0[64 * s:64 * s + 64, ds(a, 1), 128 * (i - 1):128 * (i + 1)].rearrange("p o (b q) -> p (o b) q", q=128)
                    dve.tensor_tensor(dst, tmp, o[64:128, :, 1], ALU.add).then_inc(sem("pv_ev"), 1)

                for t in range(18):
                    if attend:
                        n = 128 * (t % QB + 1)
                        v = slice(t % 2, t % 2 + 1)
                        if t < 16:
                            dve.wait_ge(sem("sc"), 16 * a + (t + 1))
                            dve.tensor_reduce(NEGM[:, v], bank(2, 2)[:, 0:n], AX.X, ALU.max, negate=True).then_inc(sem("mx"), 1)
                        if 1 <= t <= 16:
                            lo(t - 1, 0)
                        if t >= 2 and t % 2 == 1:
                            output(t - 2)
                        if t < 16:
                            dve.wait_ge(sem("exp"), 16 * a + (t + 2))
                            dve.reciprocal(RINV[:, v], RSUM[:, v]).then_inc(sem("rinv"), 1)
                            dve.wait_ge(sem("rinv"), 16 * a + (t + 1))
                            dve.tensor_scalar(PN[:, t % 2, 0:n], PE_[:, 0:n], RINV[:, v], None, ALU.mult).then_inc(sem("p"), 1)
                        if 1 <= t <= 16 and (t - 1) % QB >= 4:
                            lo(t - 1, 1)
                    if panels and t in TAKEN:
                        take(TAKEN[t])
                    if not attend and t == 4:
                        dve.wait_ge(sem("fnh"), 1)
                        dve.tensor_tensor(FNL[q96], FC[q96], FNH[q96].bitcast(F32), ALU.subtract).then_inc(sem("fnl"), 1)

            rounds(dve, fox)

            def columns(n, g_at, b_at, sc_at, sh_at):
                C = COLS[:, n]
                g, b = VEC2[:, g_at:g_at + 8], VEC2[:, b_at:b_at + 8]
                link(dve.tensor_scalar(C[:, 3], MOD[:, sc_at:sc_at + 8], 1.0, None, ALU.add))
                link(dve.tensor_tensor(C[:, 0], C[:, 3], g, ALU.mult))
                link(dve.tensor_tensor(C[:, 1], C[:, 3], b, ALU.mult))
                link(dve.tensor_tensor(C[:, 1], C[:, 1], MOD[:, sh_at:sh_at + 8], ALU.add))
                link(dve.tensor_scalar(C[:, 2], g, ALPHA, None, ALU.mult))
                link(dve.tensor_scalar(C[:, 3], b, ALPHA, None, ALU.mult))

            def gate(n, at_):
                link(dve.tensor_scalar(G1[:, n], MOD[:, at_:at_ + 8], 1.0, None, ALU.add))

            def add_up(n, m, U, ada_n=None):
                dve.wait_ge(pp_full, U + 1)
                if n % 2 == 0:
                    dve.wait_ge(sem(f"r_in{m}"), 16 * (n // 2 + 1))
                dve.scalar_tensor_tensor(out=R[:, m], in0=pp(U % 2), scalar=G1[:, n, m:m + 1], in1=R[:, m],
                                         op0=ALU.mult, op1=ALU.add).then_inc(pp_free, 1)
                if ada_n is not None:
                    ada(ada_n)
                dve.wait_ge(pp_free, U + 3)
                if m == 1:
                    link(dve.tensor_tensor(TA[:], R[:, 0], R[:, 1], ALU.add))
                elif m > 1:
                    link(dve.tensor_tensor(TA[:], TA[:], R[:, m], ALU.add))
                if m > 0:
                    dve.wait_ge(sem("sqa"), 8 * n + m + 1)
                    dve.tensor_tensor(TB[:], TB[:], SQ[:], ALU.add).then_inc(sem("sqd"), 1)
                    dve.wait_ge(sem("sqd"), 7 * n + m)

            def norm(n, last=False):
                for h in range(2):
                    v = slice(h * HALF, (h + 1) * HALF)
                    dve.wait_ge(sem("ls"), 2 * n + h + 1)
                    link(dve.scalar_tensor_tensor(out=LV[:, v], in0=bank(6 + h), scalar=1.0 / D, in1=LS[:, v], op0=ALU.mult, op1=ALU.subtract))
                    dve.tensor_scalar(LV[:, v], LV[:, v], 0.0, EPS, ALU.max, ALU.add).then_inc(sem("lv"), 1)
                for h in range(2):
                    v = slice(h * HALF, (h + 1) * HALF)
                    link(dve.tensor_scalar(LM[:, v], bank(4 + h), 1.0 / D, None, ALU.mult))
                for h in range(2):
                    v = slice(h * HALF, (h + 1) * HALF)
                    dve.wait_ge(sem("la"), 2 * n + h + 1)
                    link(dve.scalar_tensor_tensor(out=LB[:, v], in0=LM[:, v], scalar=-1.0, in1=LA[:, v], op0=ALU.mult, op1=ALU.mult))

                    for k in range(KT):
                        link(dve.tensor_tensor(R[:, k, v], R[:, k, v], LA[:, v], ALU.mult))
                        dve.tensor_tensor(R[:, k, v], R[:, k, v], LB[:, v], ALU.add).then_inc(sem("xn"), 1)
                if last:
                    return
                for k in range(KT):
                    dve.wait_ge(sem("uh"), 8 + 16 * n + 8 + k + 1)
                    dve.tensor_scalar(R[:, k], R[:, k], COLS[:, n, 2, k:k + 1], COLS[:, n, 3, k:k + 1], ALU.mult, ALU.add).then_inc(sem("rp"), 1)

            dve.wait_ge(ada_ev, 24 + 2)
            columns(0, 0, 16, 32, 24)
            gate(0, 16)
            for m in range(KT):
                add_up(0, m, U_WO + m, 24 + m)
            dve.wait_ge(ada_ev, 32 + 2)
            gate(1, 40)
            norm(0)

            def mlp_dve(layer, U0, n):
                def first(f, ada_too):
                    with dve.Fori(0, KT // 2) as r:
                        for k in range(2):
                            dve.wait_ge(sem("hh"), 8 * f + 2 * r + (32 * layer + k + 1))
                            dve.tensor_tensor(HL[:, ds(2 * r + k, 1)], (TA, TB)[k][:].unsqueeze(1),
                                              HH[:, ds(2 * r + k, 1)].bitcast(F32), ALU.subtract).then_inc(sem("hl"), 1)
                            if ada_too:
                                ada(16 * f + 2 * r + (32 + k))

                dve.wait_ge(sem("rp"), 8 * n)
                with dve.Fori(0, 3) as f:
                    first(f, layer == 0)
                    with dve.Fori(0, KT // 2) as r:
                        for k in range(2):
                            U = 16 * f + 2 * r + (U0 + 8 + k)
                            dve.wait_ge(pp_full, U + 1)
                            dve.wait_ge(pp_free, U + 2)
                            dve.scalar_tensor_tensor(out=R[:, ds(2 * r + k, 1)], in0=pp((U0 + k) % 2).unsqueeze(1),
                                                     scalar=G1[:, n, ds(2 * r + k, 1)], in1=R[:, ds(2 * r + k, 1)],
                                                     op0=ALU.mult, op1=ALU.add).then_inc(pp_free, 1)
                            if layer == 0:
                                ada(16 * f + 2 * r + (40 + k))
                first(3, False)
                if layer == 0:
                    dve.wait_ge(ada_ev, ADA_JOBS + 2)
                    columns(1, 32, 48, 56, 48)
                    columns(2, 8, 24, 80, 72)
                    gate(2, 64)
                    gate(3, 88)
                dve.wait_ge(pp_free, U0 + 56 + 2)
                for m in range(KT):
                    add_up(n, m, U0 + 56 + m)

            mlp_dve(0, P_MLP0 + U_OF_P, 1)
            norm(1)

            dve.memset(XP[:, 0:3], 0.0).then_inc(sem("xp0"), 1)
            dve.wait_ge(pp_full, P_DT + U_OF_P + 1)
            dve.tensor_scalar(DZ[q96], pp((P_DT + U_OF_P) % 2)[q96], SMALL[q96, 1:2], None, ALU.add).then_inc(pp_free, 1)
            dve.wait_ge(pp_free, P_DT + U_OF_P + 3)
            log1p_exp(1, DZ, DDE, DE, DU, DL)
            dve.wait_ge(sem("xspill1"), 16 * KT)
            link(dve.scalar_tensor_tensor(out=DTT[q96], in0=DZ[q96], scalar=0.0, in1=DL[q96], op0=ALU.max, op1=ALU.add))
            dve.wait_ge(sem("alog"), 1)
            link(dve.tensor_scalar(SMALL[q96, 4:5], SMALL[q96, 3:4], -1.0, None, ALU.mult))
            link(dve.tensor_scalar(DZ[q96], DTT[q96], SMALL[q96, 4:5], None, ALU.mult))
            for j in range(QB):
                l = slice(128 * j, 128 * j + 128)
                scan_ = dve.tensor_tensor_scan(ACS[q96, l], ONESF[q96], DZ[q96, l], 0.0, ALU.mult, ALU.add)
            link(scan_)
            acs_c = ACS[q96].rearrange("p (c l) -> p c l", l=128)
            dve.tensor_tensor(DDE[q96].rearrange("p (c l) -> p c l", l=128), acs_c[:, :, 127:128].broadcast_to([32, QB, 128]),
                              acs_c, ALU.subtract).then_inc(sem("acs"), 1)
            for n, src in enumerate((ACS, EAC)):
                dve.wait_ge(sem("rwh"), n + 1)
                dve.tensor_tensor(RWL[n][q96], src[q96], RWH[n][q96].bitcast(F32), ALU.subtract).then_inc(sem("rwl"), 1)
            dve.wait_ge(sem("dde"), 1)
            dve.tensor_tensor(DDE[q96], DDE[q96], DTT[q96], ALU.mult).then_inc(sem("dtrows"), 1)
            link(dve.memset(HS[:], 0.0))

            def ssm(it, par, panels, scan):
                g = it - 1
                gp = 1 - par
                xs, bc = XS[gp], BC[gp]
                SG, EB, TR, YB = bank(4), bank(5), bank(6), bank(7)

                def heads(v, n=128):
                    return v.rearrange("p (h n) -> p h n", n=n)

                def per_head(tab, cnk, n):
                    return tab[:, cnk, ds(4 * g, HPG)].unsqueeze(2).broadcast_to([128, HPG, n])

                def take(j):
                    if j < 4:
                        col = (it + 16, it + 24, 2 * it, 2 * it + 1)[j]
                        dve.wait_ge(sem("ct"), 4 * it + (j + 1))
                        for tap in (2, 1, 0):
                            ins = dve.scalar_tensor_tensor(out=CT[:], in0=XP[:, tap:tap + S], scalar=VEC3[:, ds(col + 32 * tap, 1)],
                                                           in1=CT[:], op0=ALU.mult, op1=ALU.add)
                            if tap:
                                ins.then_inc(sem("tap"), 1)
                                dve.wait_ge(sem("tap"), 8 * it + (2 * j + 3 - tap))
                        ins.then_inc(sem("conv"), 1)
                    if j >= 4:
                        if not (isinstance(it, int) and it == 0):
                            dve.wait_ge(sem("yout"), 32 * it)
                        dve.wait_ge(pp_free, 6 * it + (P_SSM + j + U_OF_P + 3))
                        silu(j, YR[:, par, j - 4])

                def silu(j, dst):
                    if j < 4:
                        dve.wait_ge(sem("tt"), 4 * it + (j + 1))
                    dve.scalar_tensor_tensor(out=dst, in0=TT[:], scalar=1.0, in1=CT[:], op0=ALU.add, op1=ALU.mult).then_inc(sem("silu"), 1)

                def silu_late(cnk):
                    if panels and cnk - 1 in EVICT and EVICT[cnk - 1] < 4:
                        j = EVICT[cnk - 1]
                        silu(j, BC[par][:, j] if j < 2 else XS[par][:, j - 2])

                def finish(g_, p):
                    dve.wait_ge(sem("rsa"), g_ + 1)
                    for t in range(2):
                        dve.scalar_tensor_tensor(out=YR[:, p, t], in0=YR[:, p, t], scalar=VEC2[:, ds(2 * g_ + (96 + t), 1)],
                                                 in1=RS2[:], op0=ALU.mult, op1=ALU.mult).then_inc(sem("yfin"), 1)

                for cnk in range(QB):
                    if scan:
                        l = slice(128 * cnk, 128 * cnk + 128)
                        e = 8 * g + cnk
                        if cnk == 0:
                            dve.wait_ge(sem("tables"), 3)
                            dve.wait_ge(sem("silu"), 6 * g + 7)
                        dve.wait_ge(sem("sg"), e + 1)
                        dve.tensor_tensor(ES[:], heads(SG), per_head(TAC, cnk, 128), ALU.subtract).then_inc(sem("seg"), 1)
                        silu_late(cnk)
                        dve.wait_ge(sem("bt"), e + 1)
                        dve.tensor_tensor(heads(XD[:], 64), heads(TR[:, 0:256], 64), per_head(TDT, cnk, 64), ALU.mult)
                        dve.tensor_tensor(heads(XE[:], 64), heads(TR[:, 0:256], 64), per_head(TDE, cnk, 64), ALU.mult)
                        dve.wait_ge(sem("eb"), e + 1)
                        dve.tensor_tensor(CS[:], heads(EB), bc[:, 1, l].unsqueeze(1).broadcast_to([128, HPG, 128]), ALU.mult)
                        dve.wait_ge(sem("es"), e + 1)
                        dve.tensor_tensor(MS[:], ES[:], TR[:, 384:512].unsqueeze(1).broadcast_to([128, HPG, 128]), ALU.mult).then_inc(sem("ms"), 1)
                        dve.wait_ge(sem("yps"), e + 1)
                        for h in range(HPG):
                            t, rows = h // 2, slice(64 * (h % 2), 64 * (h % 2) + 64)
                            ins = dve.scalar_tensor_tensor(out=XD[rows, 128 * t:128 * t + 128], in0=xs[rows, t, l],
                                                           scalar=DCOL[rows, ds(2 * g + t, 1)], in1=YB[rows, 128 * h:128 * h + 128],
                                                           op0=ALU.mult, op1=ALU.add)
                        ins.then_inc(sem("yd"), 1)
                        dve.wait_ge(sem("yd"), e + 1)
                        dve.tensor_tensor(YR[:, gp, :, l], YR[:, gp, :, l], heads(XD[:]), ALU.mult).then_inc(sem("yev"), 1)
                        if cnk < QB - 1:
                            dve.tensor_tensor(heads(HT[:], 64), heads(HS[:], 64), heads(EB)[:, :, 127:128].broadcast_to([128, HPG, 64]),
                                              ALU.mult).then_inc(sem("ht"), 1)
                            dve.wait_ge(sem("ht"), 7 * g + (cnk + 1))
                            dve.wait_ge(sem("st"), 7 * g + (cnk + 1))
                            dve.tensor_tensor(HS[:], HT[:], SG[:, 0:256], ALU.add).then_inc(sem("hs"), 1)
                        else:
                            dve.memset(HS[:], 0.0).then_inc(sem("hs"), 1)
                        dve.wait_ge(sem("hs"), e + 2)
                        if cnk == 0 and not (isinstance(it, int) and it == 1):
                            finish(it - 2, par)
                    if not scan:
                        silu_late(cnk)
                    if panels and cnk in EVICT:
                        take(EVICT[cnk])
                if scan:
                    dve.wait_ge(sem("ysa"), 2 * g + 2)
                    dve.tensor_tensor(SQ2[:], SQ2[:], RS2[:], ALU.add).then_inc(sem("ysq"), 1)
                    dve.wait_ge(sem("rms"), g + 1)
                    dve.tensor_scalar(RS2[:], bank(4, 2), 1.0 / 256, EPS, ALU.mult, ALU.add).then_inc(sem("rms_ev"), 1)
                if panels:
                    take(5)
                else:
                    finish(g, gp)
                if not scan:
                    dve.wait_ge(sem("tab_ps"), 1)
                    for q, tab in enumerate((TDT, TAC, TDE)):
                        dve.tensor_copy(tab[:], bank(4, 2)[:, 256 * q:256 * q + 256].rearrange("p (c h) -> p c h", h=32)).then_inc(sem("tables"), 1)

            rounds(dve, ssm)
            for m in range(KT):
                U = P_OUT + m + U_OF_P
                dve.wait_ge(pp_full, U + 1)
                dve.wait_ge(sem(f"r_in{m}"), 32)
                dve.scalar_tensor_tensor(out=R[:, m], in0=pp(U % 2), scalar=G1[:, 2, m:m + 1], in1=R[:, m],
                                         op0=ALU.mult, op1=ALU.add).then_inc(pp_free, 1)
            dve.wait_ge(pp_free, P_OUT + KT + U_OF_P + 2)
            for m in range(KT):
                add_up(2, m, P_OUT + KT + m + U_OF_P)
            norm(2)
            mlp_dve(1, P_MLP1 + U_OF_P, 3)
            norm(3, last=True)


_INPUTS = ["x", "c", "ada_w", "ada_b", "ln_mix_g", "ln_mix_b", "ln_mlp_g", "ln_mlp_b", "mlp_w1", "mlp_w2",
           "fox_w_in", "fox_b_f", "fox_w_o", "ssm_w_in", "ssm_conv_w", "ssm_conv_b", "ssm_dt_bias",
           "ssm_a_log", "ssm_d", "ssm_norm_w", "ssm_w_out"]


def kernel(**inputs):
    import numpy as _np
    import concourse.bacc as _bacc
    from concourse import mybir as _mybir
    from concourse.bass_utils import run_bass_kernel_spmd as _run

    nc = _bacc.Bacc("TRN2", target_bir_lowering=False, num_devices=1)
    arrays, args = {}, []
    for name in _INPUTS:
        a = _np.ascontiguousarray(inputs[name])
        arrays[f"in_{name}_dram"] = a
        args.append(nc.dram_tensor(f"in_{name}_dram", a.shape, _mybir.dt.from_np(a.dtype), kind="ExternalInput").ap())
    args.append(nc.dram_tensor("out_0_dram", (1, S, D), _mybir.dt.float32, kind="ExternalOutput").ap())
    build(nc, *args)
    r = _run(nc, [arrays], core_ids=[0])
    return r.results[0]["out_0_dram"]
```
